# Optimizing a Trainium2 kernel written in Bass

```python
import jax, jax.numpy as jnp
from jax import lax
import numpy as np

D_MODEL = 1024
BATCH = 1
SEQ = 256
DEPTH = 1

N_META = 16
MIX_WIDTH = D_MODEL
POOL_WIDTH = MIX_WIDTH // 2
POOL_WINDOWS = (2, 4, 8, 16)
N_POOL_GROUPS = 4
POOL_GROUP = POOL_WIDTH // N_POOL_GROUPS
GLA_HEADS = 4
GLA_VDIM = MIX_WIDTH - POOL_WIDTH
GLA_HEAD_V = GLA_VDIM // GLA_HEADS
GLA_KDIM = GLA_VDIM // 2
GLA_HEAD_K = GLA_KDIM // GLA_HEADS
GATE_RANK = 16
GATE_NORMALIZER = 16.0
CHUNK = 64
N_GROUPS = 4
EXPERTS_PER_GROUP = 4
N_EXPERTS = N_GROUPS * EXPERTS_PER_GROUP
TOP_K_IN_GROUP = 2
EXPERT_HIDDEN = D_MODEL // 4
EPS = 1e-6
IN_COLS = POOL_WIDTH + 2 * GLA_KDIM + 2 * GLA_VDIM + GATE_RANK
SPLIT_POINTS = (POOL_WIDTH,
                POOL_WIDTH + GLA_KDIM,
                POOL_WIDTH + 2 * GLA_KDIM,
                POOL_WIDTH + 2 * GLA_KDIM + GLA_VDIM,
                POOL_WIDTH + 2 * GLA_KDIM + 2 * GLA_VDIM)


def rmsnorm(x, w):
    xf = x.astype(jnp.float32)
    y = xf * lax.rsqrt(jnp.mean(xf * xf, axis=-1, keepdims=True) + EPS)
    return (y * w.astype(jnp.float32)).astype(x.dtype)

def pool_mixer(u, pool_w, pool_scale):
    B, L, _ = u.shape
    uf = u.astype(jnp.float32).reshape(B, L, N_POOL_GROUPS, POOL_GROUP)
    cs = jnp.concatenate([jnp.zeros((B, 1, N_POOL_GROUPS, POOL_GROUP), jnp.float32),
                          jnp.cumsum(uf, axis=1)], axis=1)
    t = jnp.arange(L)
    outs = []
    for g, w in enumerate(POOL_WINDOWS):
        lo = jnp.maximum(t + 1 - w, 0)
        cs_g = cs[:, :, g]
        win_sum = cs_g[:, 1:] - cs_g[:, lo]
        cnt = (t + 1 - lo).astype(jnp.float32)[None, :, None]
        outs.append(win_sum / cnt - uf[:, :, g])
    pooled = jnp.stack(outs, axis=2)
    mixed = jnp.einsum('blgc,gcd->blgd', pooled, pool_w.astype(jnp.float32))
    y = mixed.reshape(B, L, POOL_WIDTH) * pool_scale.astype(jnp.float32)
    return y.astype(u.dtype)

def gla_mixer(q, k, v, r, g_lr, w_gate_up, b_gate, gla_norm_w):
    B, L, _ = q.shape
    f32 = jnp.float32
    log_a = jax.nn.log_sigmoid(g_lr.astype(f32) @ w_gate_up.astype(f32)
                               + b_gate.astype(f32)) / GATE_NORMALIZER
    pad = CHUNK - N_META

    def heads(a, dh):
        a = jnp.pad(a.astype(f32), ((0, 0), (pad, 0), (0, 0)))
        return a.reshape(B, -1, CHUNK, GLA_HEADS, dh).transpose(0, 3, 1, 2, 4)

    qh = heads(q, GLA_HEAD_K) * (GLA_HEAD_K ** -0.5)
    kh = heads(k, GLA_HEAD_K)
    vh = heads(v, GLA_HEAD_V)
    gh = heads(log_a, GLA_HEAD_K)
    b = jnp.cumsum(gh, axis=3)
    b_last = b[:, :, :, -1:, :]
    q_t = qh * jnp.exp(b)
    k_t = kh * jnp.exp(-b)
    k_end = kh * jnp.exp(b_last - b)
    causal = jnp.tril(jnp.ones((CHUNK, CHUNK), dtype=bool))
    scores = jnp.where(causal, jnp.einsum('bhncd,bhnsd->bhncs', q_t, k_t), 0.0)
    o_intra = jnp.einsum('bhncs,bhnsv->bhncv', scores, vh)
    dS = jnp.einsum('bhncd,bhncv->bhndv', k_end, vh)
    decay = jnp.exp(b_last[:, :, :, 0, :])

    def step(S, inp):
        dS_n, dec_n = inp
        return dec_n[..., None] * S + dS_n, S

    S0 = jnp.zeros((B, GLA_HEADS, GLA_HEAD_K, GLA_HEAD_V), f32)
    _, S_start = lax.scan(step, S0, (jnp.moveaxis(dS, 2, 0), jnp.moveaxis(decay, 2, 0)))
    S_start = jnp.moveaxis(S_start, 0, 2)
    o_inter = jnp.einsum('bhncd,bhndv->bhncv', q_t, S_start)
    o = (o_intra + o_inter).transpose(0, 2, 3, 1, 4).reshape(B, -1, GLA_HEADS, GLA_HEAD_V)[:, pad:]
    o = o * lax.rsqrt(jnp.mean(o * o, axis=-1, keepdims=True) + EPS) * gla_norm_w.astype(f32)
    o = o.reshape(B, L, GLA_VDIM) * jax.nn.silu(r.astype(f32))
    return o.astype(q.dtype)

def hier_moe(x, w_rg, b_rg, w_re, b_re, w_gate, w_up, w_down):
    B, L, D = x.shape
    f32 = jnp.float32
    xt = x.reshape(-1, D)
    xf = xt.astype(f32)
    g_logits = xf @ w_rg.astype(f32) + b_rg.astype(f32)
    g_prob = jax.nn.softmax(g_logits, axis=-1)
    g_sel = jnp.argmax(g_logits, axis=-1)
    p_g = jnp.take_along_axis(g_prob, g_sel[:, None], axis=-1)
    e_logits = (xf @ w_re.astype(f32) + b_re.astype(f32)).reshape(-1, N_GROUPS, EXPERTS_PER_GROUP)
    e_logits = jnp.take_along_axis(e_logits, g_sel[:, None, None], axis=1)[:, 0]
    e_prob = jax.nn.softmax(e_logits, axis=-1)
    top_p, top_i = lax.top_k(e_prob, TOP_K_IN_GROUP)
    top_p = top_p / jnp.sum(top_p, axis=-1, keepdims=True)
    weights = p_g * top_p
    expert_id = g_sel[:, None] * EXPERTS_PER_GROUP + top_i
    combine = jnp.sum(jax.nn.one_hot(expert_id, N_EXPERTS, dtype=f32) * weights[..., None], axis=1)
    y = jnp.zeros(xf.shape, f32)
    for e in range(N_EXPERTS):
        h = jax.nn.silu(xt @ w_gate[e]) * (xt @ w_up[e])
        y = y + combine[:, e:e + 1] * (h @ w_down[e]).astype(f32)
    return y.reshape(B, L, D).astype(x.dtype)

def first_inputs(seed: int = 0) -> dict:
    key = jax.random.key(seed)
    ks = jax.random.split(key, 20)
    n = jax.random.normal
    D = D_MODEL
    return {
        "x": n(ks[0], (BATCH, SEQ, D), jnp.float32),
        "meta_tokens": n(ks[1], (N_META, D), jnp.float32),
        "norm_mix_w": 1.0 + 0.05 * n(ks[2], (DEPTH, D), jnp.float32),
        "w_in": n(ks[3], (DEPTH, D, IN_COLS), jnp.float32) * D ** -0.5,
        "w_gate_up": n(ks[4], (DEPTH, GATE_RANK, GLA_KDIM), jnp.float32) * GATE_RANK ** -0.5,
        "b_gate": 0.1 * n(ks[5], (DEPTH, GLA_KDIM), jnp.float32),
        "gla_norm_w": 1.0 + 0.05 * n(ks[6], (DEPTH, GLA_HEAD_V), jnp.float32),
        "pool_w": n(ks[7], (DEPTH, N_POOL_GROUPS, POOL_GROUP, POOL_GROUP), jnp.float32) * POOL_GROUP ** -0.5,
        "pool_scale": 1.0 + 0.05 * n(ks[8], (DEPTH, POOL_WIDTH), jnp.float32),
        "w_out": n(ks[9], (DEPTH, MIX_WIDTH, D), jnp.float32) * MIX_WIDTH ** -0.5,
        "norm_ffn_w": 1.0 + 0.05 * n(ks[10], (DEPTH, D), jnp.float32),
        "w_router_group": n(ks[11], (DEPTH, D, N_GROUPS), jnp.float32) * D ** -0.5,
        "b_router_group": 0.01 * n(ks[12], (DEPTH, N_GROUPS), jnp.float32),
        "w_router_expert": n(ks[13], (DEPTH, D, N_EXPERTS), jnp.float32) * D ** -0.5,
        "b_router_expert": 0.01 * n(ks[14], (DEPTH, N_EXPERTS), jnp.float32),
        "w_expert_gate": n(ks[15], (DEPTH, N_EXPERTS, D, EXPERT_HIDDEN), jnp.float32) * D ** -0.5,
        "w_expert_up": n(ks[16], (DEPTH, N_EXPERTS, D, EXPERT_HIDDEN), jnp.float32) * D ** -0.5,
        "w_expert_down": n(ks[17], (DEPTH, N_EXPERTS, EXPERT_HIDDEN, D), jnp.float32) * EXPERT_HIDDEN ** -0.5,
        "final_norm_w": 1.0 + 0.05 * n(ks[18], (D,), jnp.float32),
    }

def first_block(x, meta_tokens, norm_mix_w, w_in, w_gate_up, b_gate, gla_norm_w, pool_w,
              pool_scale, w_out, norm_ffn_w, w_router_group, b_router_group,
              w_router_expert, b_router_expert, w_expert_gate, w_expert_up,
              w_expert_down, final_norm_w):
    B = x.shape[0]
    meta = jnp.broadcast_to(meta_tokens[None].astype(x.dtype), (B, N_META, D_MODEL))
    h = jnp.concatenate([meta, x], axis=1)
    for l in range(DEPTH):
        u = rmsnorm(h, norm_mix_w[l])
        proj = u @ w_in[l]
        pool_v, q, k, v, r, g_lr = jnp.split(proj, SPLIT_POINTS, axis=-1)
        y_pool = pool_mixer(pool_v, pool_w[l], pool_scale[l])
        y_gla = gla_mixer(q, k, v, r, g_lr, w_gate_up[l], b_gate[l], gla_norm_w[l])
        h = h + jnp.concatenate([y_pool, y_gla], axis=-1) @ w_out[l]
        h = h + hier_moe(rmsnorm(h, norm_ffn_w[l]), w_router_group[l], b_router_group[l],
                         w_router_expert[l], b_router_expert[l], w_expert_gate[l],
                         w_expert_up[l], w_expert_down[l])
    return rmsnorm(h, final_norm_w)[:, N_META:]


DEPTH_2 = 2

GRID_W = 64
CTX_LEN = 256
HEAD_DIM = 64
MIX_WIDTH_2 = D_MODEL
A_HEADS = 6
A_KV = 2
A_WINDOW = 128
A_BLOCK = 128
B_HEADS = 4
B_KV = 2
B_BLOCK = 128
C_HEADS = 6
NA_KH = 8
NA_KW = 16
D_FF = 2816
ROPE_THETA = 10000.0
N_MOD = 9
NEG = -1e30
KV_WIDTHS = (A_KV, A_KV, B_KV, B_KV, C_HEADS, C_HEADS)
W_IN_COLS = MIX_WIDTH_2 + sum(KV_WIDTHS) * HEAD_DIM


def _rms_norm(x, g):
    xf = x.astype(jnp.float32)
    y = xf * lax.rsqrt(jnp.mean(xf * xf, axis=-1, keepdims=True) + EPS)
    return (y * g.astype(jnp.float32)).astype(x.dtype)

def _modulate(u, shift, scale):
    return u * (1.0 + scale) + shift

def _swiglu(u, w_gate, w_up, w_down):
    return (jax.nn.silu(u @ w_gate) * (u @ w_up)) @ w_down

def _axial_rope(S):
    t = jnp.arange(S)
    row = (t // GRID_W).astype(jnp.float32)
    col = (t % GRID_W).astype(jnp.float32)
    n_freq = HEAD_DIM // 4
    inv = ROPE_THETA ** (-jnp.arange(n_freq, dtype=jnp.float32) / n_freq)
    ang = jnp.concatenate([row[:, None] * inv, col[:, None] * inv], axis=-1)
    return jnp.cos(ang), jnp.sin(ang)

def _rope(x, cos, sin):
    half = HEAD_DIM // 2
    x1, x2 = x[..., :half], x[..., half:]
    cs, sn = cos[None, :, None, :], sin[None, :, None, :]
    return jnp.concatenate([x1 * cs - x2 * sn, x2 * cs + x1 * sn], axis=-1).astype(x.dtype)

def _multi_softmax(logits):
    sizes = [int(l.shape[-1]) for l in logits]
    p = jax.nn.softmax(jnp.concatenate(logits, axis=-1), axis=-1)
    return jnp.split(p, [int(s) for s in np.cumsum(sizes)[:-1]], axis=-1)

def _heads(t, n):
    return t.reshape(*t.shape[:-1], n, HEAD_DIM)

def _split_q(p):
    a = A_HEADS * HEAD_DIM
    b = B_HEADS * HEAD_DIM
    return (_heads(p[..., :a], A_HEADS), _heads(p[..., a:a + b], B_HEADS),
            _heads(p[..., a + b:MIX_WIDTH_2], C_HEADS))

def _split_kv(p):
    offs = [0]
    for w in KV_WIDTHS:
        offs.append(offs[-1] + w * HEAD_DIM)
    return [_heads(p[..., offs[i]:offs[i + 1]], KV_WIDTHS[i]) for i in range(len(KV_WIDTHS))]

def _ctx_attn(qc, kc, vc, sink=None):
    Bn, L, H, d = qc.shape
    KV = kc.shape[2]
    G = H // KV
    qg = qc.reshape(Bn, L, KV, G, d)
    s = jnp.einsum('bqkgd,blkd->bkgql', qg, kc).astype(jnp.float32) * (d ** -0.5)
    if sink is None:
        p = jax.nn.softmax(s, axis=-1)
    else:
        sink_col = jnp.broadcast_to(sink.astype(jnp.float32).reshape(1, KV, G, 1, 1), (Bn, KV, G, L, 1))
        p, _ = _multi_softmax([s, sink_col])
    out = jnp.einsum('bkgql,blkd->bqkgd', p.astype(vc.dtype), vc)
    return out.reshape(Bn, L, H * d)

def _window_attn(q, k, v, kc, vc, sink):
    Bn, S, H, d = q.shape
    KV = k.shape[2]
    G = H // KV
    nb = S // A_BLOCK
    band = 3 * A_BLOCK
    scale = d ** -0.5
    pad = ((0, 0), (A_BLOCK, A_BLOCK), (0, 0), (0, 0))
    kp, vp = jnp.pad(k, pad), jnp.pad(v, pad)
    qb = jnp.moveaxis(q.reshape(Bn, nb, A_BLOCK, KV, G, d), 1, 0)
    rel = jnp.arange(band)[None, :] - A_BLOCK - jnp.arange(A_BLOCK)[:, None]
    sink_col = jnp.broadcast_to(sink.astype(jnp.float32).reshape(1, KV, G, 1, 1), (Bn, KV, G, A_BLOCK, 1))

    def block(args):
        n, q_n = args
        start = n * A_BLOCK
        k_n = lax.dynamic_slice_in_dim(kp, start, band, axis=1)
        v_n = lax.dynamic_slice_in_dim(vp, start, band, axis=1)
        kpos = start - A_BLOCK + jnp.arange(band)
        mask = (jnp.abs(rel) <= A_WINDOW) & ((kpos >= 0) & (kpos < S))[None, :]
        s_w = jnp.einsum('bqkgd,bskd->bkgqs', q_n, k_n).astype(jnp.float32) * scale
        s_w = jnp.where(mask, s_w, NEG)
        s_c = jnp.einsum('bqkgd,blkd->bkgql', q_n, kc).astype(jnp.float32) * scale
        p_w, p_c, _ = _multi_softmax([s_w, s_c, sink_col])
        return (jnp.einsum('bkgqs,bskd->bqkgd', p_w.astype(v.dtype), v_n)
                + jnp.einsum('bkgql,blkd->bqkgd', p_c.astype(vc.dtype), vc))

    out = lax.map(block, (jnp.arange(nb), qb))
    return jnp.moveaxis(out, 0, 1).reshape(Bn, S, H * d)

def _global_attn(q, k, v, kc, vc):
    Bn, S, H, d = q.shape
    KV = k.shape[2]
    G = H // KV
    nb = S // B_BLOCK
    scale = d ** -0.5
    qb = jnp.moveaxis(q.reshape(Bn, nb, B_BLOCK, KV, G, d), 1, 0)

    def block(q_n):
        s_l = jnp.einsum('bqkgd,bskd->bkgqs', q_n, k).astype(jnp.float32) * scale
        s_c = jnp.einsum('bqkgd,blkd->bkgql', q_n, kc).astype(jnp.float32) * scale
        p_l, p_c = _multi_softmax([s_l, s_c])
        return (jnp.einsum('bkgqs,bskd->bqkgd', p_l.astype(v.dtype), v)
                + jnp.einsum('bkgql,blkd->bqkgd', p_c.astype(vc.dtype), vc))

    out = lax.map(block, qb)
    return jnp.moveaxis(out, 0, 1).reshape(Bn, S, H * d)

def _neighbourhood_attn(q, k, v, kc, vc, rpb):
    Bn, S, H, d = q.shape
    rows = S // GRID_W
    kh = min(NA_KH, rows)
    kw = NA_KW
    n_keys = kh * kw
    scale = d ** -0.5
    qg = jnp.moveaxis(q.reshape(Bn, rows, GRID_W, H, d), 1, 0)
    kg = k.reshape(Bn, rows, GRID_W, H, d)
    vg = v.reshape(Bn, rows, GRID_W, H, d)
    cols = np.arange(GRID_W)
    col_idx = np.clip(cols - kw // 2, 0, GRID_W - kw)[:, None] + np.arange(kw)[None, :]
    dc = col_idx - cols[:, None] + NA_KW - 1
    rpb_col = rpb[:, :, dc]

    def gather(t, rs):
        t_rows = lax.dynamic_slice_in_dim(t, rs, kh, axis=1)
        t_nb = t_rows[:, :, col_idx]
        return jnp.transpose(t_nb, (0, 2, 1, 3, 4, 5)).reshape(Bn, GRID_W, n_keys, H, d)

    def block(args):
        r, q_r = args
        rs = jnp.clip(r - kh // 2, 0, rows - kh)
        dr = rs + jnp.arange(kh) - r + NA_KH - 1
        bias = jnp.transpose(jnp.take(rpb_col, dr, axis=1), (0, 2, 1, 3)).reshape(H, GRID_W, n_keys)
        k_nb, v_nb = gather(kg, rs), gather(vg, rs)
        s_n = jnp.einsum('bwhd,bwnhd->bhwn', q_r, k_nb).astype(jnp.float32) * scale + bias.astype(jnp.float32)
        s_c = jnp.einsum('bwhd,blhd->bhwl', q_r, kc).astype(jnp.float32) * scale
        p_n, p_c = _multi_softmax([s_n, s_c])
        return (jnp.einsum('bhwn,bwnhd->bwhd', p_n.astype(v.dtype), v_nb)
                + jnp.einsum('bhwl,blhd->bwhd', p_c.astype(vc.dtype), vc))

    out = lax.map(block, (jnp.arange(rows), qg))
    return jnp.moveaxis(out, 0, 1).reshape(Bn, S, H * d)

def second_inputs(seed: int = 0) -> dict:
    key = jax.random.key(seed)
    ks = jax.random.split(key, 24)
    f32 = jnp.float32
    D, F = D_MODEL, D_FF

    def nrm(k, shape, s):
        return jax.random.normal(k, shape, f32) * s

    def gain(k, shape):
        return 1.0 + 0.02 * jax.random.normal(k, shape, f32)

    return {
        "x": nrm(ks[0], (BATCH, SEQ, D), 1.0),
        "c": nrm(ks[1], (BATCH, D), 1.0),
        "ctx": nrm(ks[2], (BATCH, CTX_LEN, D), 1.0),
        "c_ctx": nrm(ks[3], (D,), 1.0),
        "w_ada": nrm(ks[4], (DEPTH_2, D, N_MOD * D), 0.5 * D ** -0.5),
        "b_ada": nrm(ks[5], (DEPTH_2, N_MOD * D), 0.02),
        "norm_ffn1": gain(ks[6], (DEPTH_2, D)),
        "w_ffn1_gate": nrm(ks[7], (DEPTH_2, D, F), D ** -0.5),
        "w_ffn1_up": nrm(ks[8], (DEPTH_2, D, F), D ** -0.5),
        "w_ffn1_down": nrm(ks[9], (DEPTH_2, F, D), F ** -0.5),
        "norm_mix": gain(ks[10], (DEPTH_2, D)),
        "w_in": nrm(ks[11], (DEPTH_2, D, W_IN_COLS), D ** -0.5),
        "q_norm_glob": gain(ks[12], (DEPTH_2, HEAD_DIM)),
        "k_norm_glob": gain(ks[13], (DEPTH_2, HEAD_DIM)),
        "sink_win": nrm(ks[14], (DEPTH_2, A_HEADS), 0.5),
        "rpb_nbr": nrm(ks[15], (DEPTH_2, C_HEADS, 2 * NA_KH - 1, 2 * NA_KW - 1), 0.1),
        "w_out": nrm(ks[16], (DEPTH_2, MIX_WIDTH_2, D), MIX_WIDTH_2 ** -0.5),
        "norm_ffn2": gain(ks[17], (DEPTH_2, D)),
        "w_ffn2_gate": nrm(ks[18], (DEPTH_2, D, F), D ** -0.5),
        "w_ffn2_up": nrm(ks[19], (DEPTH_2, D, F), D ** -0.5),
        "w_ffn2_down": nrm(ks[20], (DEPTH_2, F, D), F ** -0.5),
        "norm_final": gain(ks[21], (D,)),
    }

def second_block(x, c, ctx, c_ctx, w_ada, b_ada, norm_ffn1, w_ffn1_gate, w_ffn1_up, w_ffn1_down,
              norm_mix, w_in, q_norm_glob, k_norm_glob, sink_win, rpb_nbr, w_out,
              norm_ffn2, w_ffn2_gate, w_ffn2_up, w_ffn2_down, norm_final):
    S = x.shape[1]
    cos, sin = _axial_rope(S)
    h, hc = x, ctx
    for l in range(DEPTH_2):
        last = l == DEPTH_2 - 1
        mod_x = (jax.nn.silu(c) @ w_ada[l] + b_ada[l])[:, None, :]
        mod_c = jax.nn.silu(c_ctx) @ w_ada[l] + b_ada[l]
        sh1, sc1, g1, shm, scm, gm, sh2, sc2, g2 = jnp.split(mod_x, N_MOD, axis=-1)
        csh1, csc1, cg1, cshm, cscm, cgm, csh2, csc2, cg2 = jnp.split(mod_c, N_MOD, axis=-1)

        h = h + 0.5 * g1 * _swiglu(_modulate(_rms_norm(h, norm_ffn1[l]), sh1, sc1),
                                   w_ffn1_gate[l], w_ffn1_up[l], w_ffn1_down[l])
        hc = hc + 0.5 * cg1 * _swiglu(_modulate(_rms_norm(hc, norm_ffn1[l]), csh1, csc1),
                                      w_ffn1_gate[l], w_ffn1_up[l], w_ffn1_down[l])

        u = _modulate(_rms_norm(h, norm_mix[l]), shm, scm)
        uc = _modulate(_rms_norm(hc, norm_mix[l]), cshm, cscm)
        p = u @ w_in[l]
        q_w, q_g, q_n = _split_q(p[..., :MIX_WIDTH_2])
        k_w, v_w, k_g, v_g, k_n, v_n = _split_kv(p[..., MIX_WIDTH_2:])
        if last:
            kv_c = uc @ w_in[l][:, MIX_WIDTH_2:]
        else:
            pc = uc @ w_in[l]
            cq_w, cq_g, cq_n = _split_q(pc[..., :MIX_WIDTH_2])
            kv_c = pc[..., MIX_WIDTH_2:]
        ck_w, cv_w, ck_g, cv_g, ck_n, cv_n = _split_kv(kv_c)

        q_g = _rms_norm(q_g, q_norm_glob[l])
        k_g = _rms_norm(k_g, k_norm_glob[l])
        ck_g = _rms_norm(ck_g, k_norm_glob[l])
        q_w, k_w = _rope(q_w, cos, sin), _rope(k_w, cos, sin)
        q_g, k_g = _rope(q_g, cos, sin), _rope(k_g, cos, sin)

        y_w = _window_attn(q_w, k_w, v_w, ck_w, cv_w, sink_win[l])
        y_g = _global_attn(q_g, k_g, v_g, ck_g, cv_g)
        y_n = _neighbourhood_attn(q_n, k_n, v_n, ck_n, cv_n, rpb_nbr[l])
        h = h + gm * (jnp.concatenate([y_w, y_g, y_n], axis=-1) @ w_out[l])

        if not last:
            cq_g = _rms_norm(cq_g, q_norm_glob[l])
            yc = jnp.concatenate([_ctx_attn(cq_w, ck_w, cv_w, sink_win[l]),
                                  _ctx_attn(cq_g, ck_g, cv_g),
                                  _ctx_attn(cq_n, ck_n, cv_n)], axis=-1)
            hc = hc + cgm * (yc @ w_out[l])

        h = h + 0.5 * g2 * _swiglu(_modulate(_rms_norm(h, norm_ffn2[l]), sh2, sc2),
                                   w_ffn2_gate[l], w_ffn2_up[l], w_ffn2_down[l])
        if not last:
            hc = hc + 0.5 * cg2 * _swiglu(_modulate(_rms_norm(hc, norm_ffn2[l]), csh2, csc2),
                                          w_ffn2_gate[l], w_ffn2_up[l], w_ffn2_down[l])
    return _rms_norm(h, norm_final)


def setup_inputs(seed=0):
    out = dict(first_inputs(seed))
    for name, value in second_inputs(seed + 1).items():
        if name != "x":
            out[name + "_2"] = value
    return out


def reference(
    x, meta_tokens, norm_mix_w, w_in, w_gate_up, b_gate, gla_norm_w, pool_w, pool_scale, w_out,
    norm_ffn_w, w_router_group, b_router_group, w_router_expert, b_router_expert, w_expert_gate,
    w_expert_up, w_expert_down, final_norm_w, c_2, ctx_2, c_ctx_2, w_ada_2, b_ada_2,
    norm_ffn1_2, w_ffn1_gate_2, w_ffn1_up_2, w_ffn1_down_2, norm_mix_2, w_in_2, q_norm_glob_2,
    k_norm_glob_2, sink_win_2, rpb_nbr_2, w_out_2, norm_ffn2_2, w_ffn2_gate_2, w_ffn2_up_2,
    w_ffn2_down_2, norm_final_2,
):
    x = first_block(
        x, meta_tokens, norm_mix_w, w_in, w_gate_up, b_gate, gla_norm_w, pool_w, pool_scale,
        w_out, norm_ffn_w, w_router_group, b_router_group, w_router_expert, b_router_expert,
        w_expert_gate, w_expert_up, w_expert_down, final_norm_w,
    )
    return second_block(
        x, c_2, ctx_2, c_ctx_2, w_ada_2, b_ada_2, norm_ffn1_2, w_ffn1_gate_2, w_ffn1_up_2,
        w_ffn1_down_2, norm_mix_2, w_in_2, q_norm_glob_2, k_norm_glob_2, sink_win_2, rpb_nbr_2,
        w_out_2, norm_ffn2_2, w_ffn2_gate_2, w_ffn2_up_2, w_ffn2_down_2, norm_final_2,
    )


_drawn_inputs = setup_inputs


def setup_inputs(seed=0):
    import zlib

    import numpy as np

    out = dict(_drawn_inputs(seed))
    spreads = {}
    factors = {'b_router_group': 6.407,
     'b_router_expert': 8.0,
     'b_ada_2': 2.781,
     'norm_ffn1_2': 8.0,
     'norm_mix_2': 8.0,
     'q_norm_glob_2': 8.0,
     'k_norm_glob_2': 8.0,
     'sink_win_2': 8.0,
     'rpb_nbr_2': 8.0,
     'norm_ffn2_2': 8.0,
     'norm_final_2': 2.821}
    for name, (base, spread) in spreads.items():
        noise = np.random.default_rng([zlib.crc32(name.encode()), seed]).standard_normal(out[name].shape)
        drawn = base * np.exp(spread * noise) if base else spread * noise
        out[name] = __import__('jax').numpy.asarray(drawn.astype(out[name].dtype))
    for name, factor in factors.items():
        out[name] = (out[name] * factor).astype(out[name].dtype)
    return out
```

```python
from contextlib import ExitStack

import numpy as np
import concourse.bass as bass
from concourse import mybir

ALU = mybir.AluOpType
ACT = mybir.ActivationFunctionType
F32 = mybir.dt.float32
F32R = mybir.dt.float32r
AX_X = mybir.AxisListType.X

P = 128
D = 1024
KD = D // P
N_META, SEQ, CTX = 16, 256, 256
T1 = N_META + SEQ
T2 = SEQ + CTX
EPS = 1e-6
CHUNKS = [(0, N_META)] + [(N_META + 64 * n, 64) for n in range(SEQ // 64)]
WINDOWS = (2, 4, 8, 16)
PAD = 16
N_GROUPS, PER_GROUP = 4, 4
N_EXPERTS = N_GROUPS * PER_GROUP
HID = D // 4
MOE_F = N_EXPERTS * HID // P
FFN_F = 2816 // P
HD = 64
GRID_W, NA_KH, NA_KW = 64, 8, 16
GRID_H = SEQ // GRID_W
RPB_W = 2 * NA_KW - 1
RPB_H = 2 * NA_KH - 1
NEG = -1e30
A_HEADS, B_HEADS, C_HEADS = 6, 4, 6
HEADS = A_HEADS + B_HEADS + C_HEADS
KA, VA, KB, VB, KC, VC = 8, 9, 10, 11, 12, 15
V_TILES = [VA, VB, VC, VC + 1, VC + 2]
PROJ2 = 18
ROPE_TILES = [0, 1, 2, KA, 3, 4, KB]
NORM_TILES = [3, 4, KB]
UNIT = 16 * P
ADA_COLS = 512
ADA_CHUNKS = 9 * D // ADA_COLS

VEC = {}
for _name, _rows in (("c", 8), ("c_ctx", 8), ("norm_mix", 8), ("norm_ffn", 8), ("final", 8), ("pool_scale", 4),
                     ("gla_norm", 1), ("b_gate", 2), ("ffn1", 16), ("mix", 16), ("ffn2", 16), ("final2", 8),
                     ("q_norm", 2), ("k_norm", 2)):
    VEC[_name] = (sum(n for _, n in VEC.values()), _rows)
VEC_ROWS = sum(n for _, n in VEC.values())


def shape_constants():
    p = np.arange(P)
    base = np.zeros((P, 264), np.float32)
    base[:, 0:128] = np.eye(P)
    base[:, 128:256] = 1.0 / D
    base[:, 256] = 1.0
    base[:, 257] = EPS
    base[:, 258:262] = [4, 3, 2, 1]
    block = (p[:, None] // HD == p[None, :] // HD) / HD
    half = HD // 2
    rot = np.zeros((P, P))
    for m in range(P):
        if m % HD < half:
            rot[m + half, m] = -1.0
        else:
            rot[m - half, m] = 1.0
    t = np.arange(SEQ)
    n_freq = HD // 4
    inv = np.float32(10000.0) ** (-np.arange(n_freq, dtype=np.float32) / n_freq)
    ang = np.concatenate([(t // GRID_W).astype(np.float32)[:, None] * inv,
                          (t % GRID_W).astype(np.float32)[:, None] * inv], axis=-1)
    cos, sin = np.cos(ang).T[p % half], np.sin(ang).T[p % half]
    q = np.arange(2)[None, :, None] * P + p[:, None, None]
    win = np.zeros((P, 2, T2))
    win[:, :, :SEQ] = np.where(np.abs(np.arange(SEQ)[None, None, :] - q) <= 128, 0.0, NEG)
    col = np.clip(p % GRID_W - NA_KW // 2, 0, GRID_W - NA_KW)[:, None]
    key = (t % GRID_W)[None, :]
    nbr = np.where((key >= col) & (key < col + NA_KW), 0.0, NEG)
    mirror = (p[:, None] == (p[None, :] // GRID_W) * GRID_W + GRID_W - 1 - p[None, :] % GRID_W)
    att = np.concatenate([block, rot, cos, sin, win.reshape(P, -1), nbr, mirror], axis=1).astype(np.float32)
    tok = np.arange(T1)
    cnt = np.stack([1.0 / np.minimum(tok + 1, w) for w in WINDOWS]).astype(np.float32)
    return base, att, np.broadcast_to(cnt.reshape(1, -1), (P, 4 * T1)).copy()


class Signal:

    def __init__(self, sem, base):
        self.sem, self.base = sem, base

    def at(self, n):
        return self.base + n


def repeat(eng, n, body):
    if n <= 3:
        for i in range(n):
            body(i)
        return
    body(0)
    with eng.Fori(1, n - 1) as i:
        body(i)
    body(n - 1)


def program(nc, a, out):
    with ExitStack() as ctx:
        counted = {}

        def sem(name):
            return ctx.enter_context(nc.semaphore(name))

        def signal(role, total):
            if role not in counted:
                counted[role] = [sem(role), 0]
            s, base = counted[role]
            counted[role][1] += total
            return Signal(s, base)

        def need(eng, sig, n=None):
            v = sig.at(n)
            if isinstance(v, int) and v <= 0:
                return
            eng.wait_ge(sig.sem, v)

        def sb(name, shape, dt=F32):
            return ctx.enter_context(nc.sbuf_tensor(name, shape, dt))

        start = (nc.sbuf_base + 31) // 32 * 32
        region_bytes = 4 * 2 * FFN_F * T2
        nc.alloc_sbuf_tensor("region", [P, region_bytes // 4 + 8], F32)
        raw = sb("raw", [P, 2, UNIT])
        w_hi = sb("w_hi", [P, 2, UNIT], F32R)
        w_lo = sb("w_lo", [P, 2, UNIT], F32R)
        u_hi = sb("u_hi", [P, KD, T2], F32R)
        u_lo = sb("u_lo", [P, KD, T2], F32R)
        h1 = sb("h1", [P, KD, T1])
        h2 = sb("h2", [P, KD, T2])
        ada_w = sb("ada_w", [P, 2, 2, ADA_COLS])
        ada_acc = sb("ada_acc", [P, 2, ADA_COLS])
        rstd = sb("rstd", [P, T2])
        tmp_a = sb("tmp_a", [P, 2, T2])
        tmp_b = sb("tmp_b", [P, 2, T2])
        base = sb("base", [P, 264])
        vec = sb("vec", [P, VEC_ROWS])
        b_ada = sb("b_ada", [P, 144, 2])
        mod = sb("mod", [P, 144, 2])
        sc_c = sb("sc_c", [P, KD, 2])
        coef = sb("coef", [P, KD, 2])
        gate = sb("gate", [P, KD, 2])
        ident, ones_d = base[:, 0:128], base[:, 128:256]
        one, eps, rank = base[:, 256:257], base[:, 257:258], base[:, 258:262]
        ps = ctx.enter_context(nc.psum_tensor("ps", [P, 8, 512], F32))

        R4_at = {}

        def carve(names):
            at, got = start, {}
            R4_at.clear()
            for name, shape, dt in names:
                size = 4 * int(np.prod(shape[1:]))
                got[name] = nc.alloc_sbuf_tensor_at(name, shape, dt, offset=at)
                R4_at[name] = at
                at += (size + 31) // 32 * 32
            assert at - start <= region_bytes, (at - start, names)
            return got

        R0 = carve([("x_rows", [P, 2, D], F32), ("meta_rows", [N_META, D], F32), ("ctx_rows", [P, 2, D], F32),
                    ("vec_rows", [VEC_ROWS, P], F32), ("bada_rows", [72, 2, P], F32)])
        R1 = carve([("proj1", [P, 16, T1], F32), ("glr_raw", [P, KD, P], F32), ("glr_hi", [P, KD, P], F32R),
                    ("glr_lo", [P, KD, P], F32R), ("glr", [P, T1], F32), ("wgu", [16, 256], F32),
                    ("win_a", [P, 4, PAD + T1], F32), ("win_b", [P, 4, PAD + T1], F32), ("cnt", [P, 4, T1], F32),
                    ("poolw", [P, 4, P], F32), ("lga", [P, 2, T1], F32), ("lgb", [P, 2, T1], F32),
                    ("qz", [P, 4, T1], F32), ("kt", [P, 2, T1], F32), ("kend", [P, 2, T1], F32),
                    ("v_tok", [64, 5, 512], F32), ("k_tok", [64, 5, 256], F32), ("sT", [64, 2, 4, 64], F32),
                    ("S", [P, 4, P], F32)])
        RG = carve([("g_pad", [P, 16, T1], F32), ("oT", [P, 4, T1], F32)])
        R2 = carve([("hm_hi", [P, MOE_F, T1], F32R), ("hm_lo", [P, MOE_F, T1], F32R), ("comb", [P, N_EXPERTS, T1], F32)])
        RR = carve([("wr", [P, KD, 20], F32), ("wr_hi", [P, KD, 20], F32R), ("wr_lo", [P, KD, 20], F32R),
                    ("rb", [P, 20], F32), ("lg", [P, 3, 20], F32), ("r4a", [P, 3, 4], F32), ("r4b", [P, 3, 4], F32),
                    ("r4c", [P, 3, 4], F32), ("oh_g", [P, 3, 4], F32), ("r1a", [P, 3], F32), ("r1b", [P, 3], F32),
                    ("r1c", [P, 3], F32), ("pg", [P, 3], F32), ("r16", [P, 3, 16], F32), ("oh1", [P, 3, 4], F32),
                    ("prob", [P, 3, 4], F32), ("combT", [16, T1], F32)])
        R3 = carve([("hf_hi", [P, FFN_F, T2], F32R), ("hf_lo", [P, FFN_F, T2], F32R)])
        R4 = carve([("proj2", [P, PROJ2, T2], F32), ("k_sw", [P, 2, T2], F32), ("vt", [P, 5, 4, P], F32),
                    ("s", [P, 2, 2, T2], F32), ("pT", [P, 2, 4, 256], F32), ("bias_c", [P, 2, C_HEADS, SEQ], F32),
                    ("att", [P, 2176], F32), ("sink", [P, A_HEADS], F32), ("st", [P, 2, 8], F32)])
        bias_rev = nc.alloc_sbuf_tensor_at("bias_rev", [P, 2, C_HEADS * SEQ], F32, offset=R4_at["s"])
        RO = carve([("o_rows", [P, 2, D], F32)])
        x_rows, meta_rows, ctx_rows, vec_rows, bada_rows = R0.values()
        (proj1, glr_raw, glr_hi, glr_lo, glr, wgu, win_a, win_b, cnt, poolw, lga, lgb, qz, kt, kend, v_tok, k_tok,
         sT, S) = R1.values()
        oT = RG["oT"]
        hm_hi, hm_lo, comb = R2.values()
        wr, wr_hi, wr_lo, rb, lg, r4a, r4b, r4c, oh_g, r1a, r1b, r1c, pg, r16, oh1, prob, combT = RR.values()
        hf_hi, hf_lo = R3.values()
        proj2, k_sw, vt, s, pT, bias_c, att, sink, st = R4.values()
        o_rows = RO["o_rows"]
        bd, rot = att[:, 0:128], att[:, 128:256]
        cos, sin = att[:, 256:512], att[:, 512:768]
        win_mask = att[:, 768:1792].rearrange("p (q k) -> p q k", q=2)
        nbr_mask, mirror = att[:, 1792:2048], att[:, 2048:2176]

        stream = []

        def streamed(name, units, groups, elems):
            u0 = sum(x["units"] for x in stream)
            g0 = sum(x["groups"] for x in stream)
            d = dict(name=name, units=units, groups=groups, elems=elems, u0=u0, g0=g0)
            stream.append(d)
            return d

        st_in1 = streamed("in1", 8, 8, UNIT)
        st_out1 = streamed("out1", 4, 4, UNIT)
        st_moe_a = streamed("moe_a", MOE_F, MOE_F, UNIT)
        st_moe_b = streamed("moe_b", 16, 8, UNIT)
        layers = []
        for l in range(2):
            layers.append(dict(
                f1a=streamed("f1a", FFN_F, FFN_F, UNIT), f1b=streamed("f1b", 16, 8, 11 * P),
                q=streamed("q", 4, 4, UNIT), kv=streamed("kv", 5, 5, UNIT), out=streamed("out", 4, 4, UNIT),
                f2a=streamed("f2a", FFN_F, FFN_F, UNIT), f2b=streamed("f2b", 16, 8, 11 * P)))
        elems_of = [x["elems"] for x in stream for _ in range(x["units"])]
        N_UNITS = len(elems_of)

        def end_of(stg):
            return stg["g0"] + stg["groups"]

        raw_full = [sem("raw_full_0"), sem("raw_full_1")]
        hi_done = signal("hi_done", 0)
        lo_done = signal("lo_done", 0)
        unit_done = signal("unit_done", 0)
        acc_free = signal("acc_free", 0)
        ada_full = [sem("ada_full_0"), sem("ada_full_1")]
        ada_mac = signal("ada_mac", 0)
        ada_sum = signal("ada_sum", 0)
        mod_done = signal("mod_done", 0)
        dve_chain = signal("dve_chain", 0)
        act_chain = signal("act_chain", 0)
        pool_chain = signal("pool_chain", 0)
        pe_chain = signal("pe_chain", 0)

        ld_rows, ld_x, ld_ctx = sem("ld_rows"), sem("ld_x"), sem("ld_ctx")
        ld_small = sem("ld_small")
        ld_router, ld_att, st_out = sem("ld_router"), sem("ld_att"), sem("st_out")
        N_ROWS = 1 + len(VEC) + 2 + 2

        norms = []
        for name in ("mix1", "ffn1", "end1", "l0a", "l0b", "l0c", "l1a", "l1b", "l1c", "end2"):
            norms.append(dict(name=name, sq=signal("norm_sq", 8), ms=signal("norm_ms", 8), root=signal("norm_root", 1),
                              rstd=signal("norm_rstd", 1), t=signal("norm_t", 8), w=signal("norm_w", 8),
                              hi=signal("norm_hi", 0 if "end" in name else 8),
                              lo=signal("norm_lo", 0 if "end" in name else 8)))
        norm_of = {n["name"]: n for n in norms}

        def ffn_signals(n, weighted=False):
            return dict(silu=signal("silu", n), comb=signal("weighted", n if weighted else 0), hi=signal("hidden_hi", n),
                        lo=signal("hidden_lo", n))

        moe_sig = ffn_signals(MOE_F, True)
        ffn_sig = [[ffn_signals(FFN_F), ffn_signals(FFN_F)] for _ in range(2)]
        for l in range(2):
            layers[l]["sig"] = ffn_sig[l]

        turned = signal("turned", 12)
        rows_out = signal("rows_out", 12)
        y_ready = [signal("y_ready", 8)]
        ev = {k: sem("ev_" + k) for k in (
            "low_zero", "low_split", "low_sum", "low_out", "win_zero", "windows", "z_sum", "z_ln", "b_sum", "exps",
            "keys", "pooled_sum", "pooled_out", "chunk_turned", "chunk_rows", "scores", "scores_out", "causal",
            "o_sum", "o_out", "chunk_state", "state", "silu_r", "o_sq", "o_ms", "o_root", "r_split", "logits", "g_shift", "g_exp",
            "e_shift", "e_exp", "shares", "shares_turned", "shares_out", "share_sum", "share_out")}

        def done(eng, name, n=1):
            eng.wait_ge(ev[name], n)

        def items(l):
            it = [(n, 0, 0, T2) for n in range(HEADS)]
            if l == 0:
                it += [(n, SEQ, SEQ, CTX) for n in range(HEADS)]
            return it

        attn = []
        for l in range(2):
            n = len(items(l))
            attn.append(dict(
                items=items(l), pre_pe=signal("at_pre_pe", 15), pre_act=signal("at_pre_act", 12),
                pre_dve=signal("at_pre_dve", 27),
                bias=signal("at_bias", 6), bias_out=signal("at_bias_out", 6), scores=signal("at_scores", n), logits=signal("at_logits", n),
                exped=signal("at_exped", n), probs=signal("at_probs", n), turned=signal("at_turned", n),
                pt=signal("at_pt", n), o=signal("at_o", n), yhi=signal("at_yhi", n), ylo=signal("at_ylo", n)))

        BIAS_BANKS = [0, 1, 2, 3, 5, 0]

        def kind(n):
            return "A" if n < A_HEADS else "B" if n < A_HEADS + B_HEADS else "C"

        def key_tile(n):
            off = HD * (n % 2)
            if kind(n) == "C":
                m = n - A_HEADS - B_HEADS
                return proj2[off:off + HD, KC + m // 2, :]
            kv = n // 3 if kind(n) == "A" else (n - A_HEADS) // 2
            which = 0 if kind(n) == "A" else 1
            if HD * kv == off:
                return proj2[off:off + HD, KA if which == 0 else KB, :]
            return k_sw[off:off + HD, which, :]

        def value_cols(n, j):
            if kind(n) == "A":
                t, kv = 0, n // 3
            elif kind(n) == "B":
                t, kv = 1, (n - A_HEADS) // 2
            else:
                m = n - A_HEADS - B_HEADS
                t, kv = 2 + m // 2, m % 2
            return vt[:, t, j, HD * kv:HD * kv + HD]

        ADA = {"moe_b": (0, 1), "f1a": (4, 2), "f1b": (14, 1), "f2a": (18, 2), "f2b": (28, 2)}

        def ada_plan(chunks):
            if chunks == 0:
                return [([], None)] * 4
            if chunks == 1:
                return [([(0, j)], -1 if j == 0 else None) for j in range(4)]
            return [([(j // 2, 2 * (j % 2)), (j // 2, 2 * (j % 2) + 1)], {0: -1, 2: 0}.get(j)) for j in range(4)]

        block = ctx.enter_context(nc.Block())

        @block.sync
        def _(sp):
            def rows(dst, src, s):
                sp.dma_start(dst, src).then_inc(s, 16)

            rows(base[:, :], a["base"], ld_rows)
            for name, src in a["vec_src"]:
                r0, n = VEC[name]
                if name in ("q_norm", "k_norm"):
                    rows(vec_rows[r0:r0 + n, 0:HD], src, ld_rows)
                    rows(vec_rows[r0:r0 + n, HD:2 * HD], src, ld_rows)
                else:
                    rows(vec_rows[r0:r0 + n, :], src, ld_rows)
            for l in range(2):
                rows(bada_rows[:, l, :], a["b_ada_2"][l].rearrange("(r c) -> r c", c=P), ld_rows)
            rows(x_rows[:, :, :], a["x"][0].rearrange("(t p) d -> p t d", p=P), ld_x)
            rows(meta_rows[:, :], a["meta_tokens"], ld_x)
            rows(ctx_rows[:, :, :], a["ctx_2"][0].rearrange("(t p) d -> p t d", p=P), ld_x)

            def unit(u, slot, parts):
                need(sp, hi_done, u - 1)
                need(sp, lo_done, u - 1)
                for dst, src in parts(raw[:, slot, :]):
                    sp.dma_start(dst, src).then_inc(raw_full[slot], 16)

            def linear(stg, w, col0=0):
                wv = w.rearrange("(k p) n -> p k n", p=P)
                for i in range(stg["units"]):
                    def parts(r, i=i):
                        v = r.rearrange("p (k n) -> p k n", k=KD)
                        c = col0 + 2 * P * i
                        return [(v[:, 0:4, :], wv[:, 0:4, c:c + 2 * P]), (v[:, 4:8, :], wv[:, 4:8, c:c + 2 * P])]
                    unit(stg["u0"] + i, (stg["u0"] + i) % 2, parts)

            def gate_up(stg, src_of, n_units):
                def step(i, j):
                    u = stg["u0"] + 4 * i + j
                    def parts(r):
                        v = r.rearrange("p (m k n) -> p m k n", m=2, k=KD)
                        g, up = src_of(i, j)
                        return [(v[:, 0], g), (v[:, 1], up)]
                    unit(u, (stg["u0"] + j) % 2, parts)
                def body(i):
                    for j in range(4):
                        step(i, j)
                repeat(sp, n_units // 4, body)
                for j in range(n_units % 4):
                    step(n_units // 4, j)

            def down(stg, w, kt2):
                wv = w.rearrange("(k p) n -> p k n", p=P)
                half = (kt2 + 1) // 2
                def body(i):
                    for j in range(4):
                        u = stg["u0"] + 4 * i + j
                        def parts(r, j=j):
                            v = r.rearrange("p (k n) -> p k n", n=P)
                            k0 = kt2 * (j % 2)
                            cols = bass.ds(i * (2 * P) + P * (j // 2), P)
                            return [(v[:, 0:half, :], wv[:, k0:k0 + half, cols]),
                                    (v[:, half:kt2, :], wv[:, k0 + half:k0 + kt2, cols])]
                        unit(u, (stg["u0"] + j) % 2, parts)
                repeat(sp, 4, body)

            linear(st_in1, a["w_in"][0])
            sp.wait_ge(rows_out.sem, rows_out.at(12))
            done(sp, "low_zero")
            sp.dma_start(glr_raw[:, :, 0:16], a["w_in"][0].rearrange("(k p) n -> p k n", p=P)[:, :, 2048:2064]).then_inc(ld_small, 16)
            sp.dma_start(wgu[:, :], a["w_gate_up"][0]).then_inc(ld_small, 16)
            sp.dma_start(cnt[:, :, :], a["cnt"].rearrange("p (g t) -> p g t", g=4)).then_inc(ld_small, 16)
            sp.dma_start(poolw[:, :, :], a["pool_w"][0].rearrange("g c d -> c g d")).then_inc(ld_small, 16)
            linear(st_out1, a["w_out"][0])
            sp.wait_ge(y_ready[0].sem, y_ready[0].at(8))
            wrv = wr[:, :, :]
            sp.dma_start(wrv[:, :, 0:4], a["w_router_group"][0].rearrange("(k p) n -> p k n", p=P)).then_inc(ld_router, 16)
            sp.dma_start(wrv[:, :, 4:20], a["w_router_expert"][0].rearrange("(k p) n -> p k n", p=P)).then_inc(ld_router, 16)
            sp.dma_start(rb[:, 0:4], a["b_router_group"][0:1, :].to_broadcast([P, 4])).then_inc(ld_router, 16)
            sp.dma_start(rb[:, 4:20], a["b_router_expert"][0:1, :].to_broadcast([P, 16])).then_inc(ld_router, 16)

            def experts(i, j):
                got = []
                for w in (a["w_expert_gate"], a["w_expert_up"]):
                    wv = w[0].rearrange("e (k p) n -> p e k n", p=P)
                    v = wv[:, bass.ds(2 * i + j // 2, 1), :, P * (j % 2):P * (j % 2) + P]
                    got.append(v.rearrange("p o k n -> p (o k) n"))
                return got
            gate_up(st_moe_a, experts, MOE_F)
            down(st_moe_b, a["w_expert_down"][0].rearrange("e f d -> (e f) d"), 16)
            for l in range(2):
                L = layers[l]

                def ffn(n):
                    def cols(i, j):
                        c = bass.ds(i * (4 * P) + P * j, P)
                        return [a[f"w_ffn{n}_{m}_2"][l].rearrange("(k p) n -> p k n", p=P)[:, :, c] for m in ("gate", "up")]
                    gate_up(L[f"f{n}a"], cols, FFN_F)
                    down(L[f"f{n}b"], a[f"w_ffn{n}_down_2"][l], 11)
                ffn(1)
                linear(L["q"], a["w_in_2"][l], 0)
                linear(L["kv"], a["w_in_2"][l], D)
                sp.wait_ge(acc_free.sem, L["q"]["g0"])
                sp.dma_start(att[:, :], a["att"]).then_inc(ld_att, 16)
                sp.dma_start(sink[:, :], a["sink_win_2"][l:l + 1, :].to_broadcast([P, A_HEADS])).then_inc(ld_att, 16)
                for r in range(GRID_H):
                    rp = a["rpb_nbr_2"]
                    off = (l * C_HEADS * RPB_H + NA_KH - 1 - r) * RPB_W + NA_KW - 1 - (GRID_W - 1)
                    p0 = GRID_W * (r % 2)
                    for h in range(C_HEADS):
                        src = bass.AP(rp.tensor, off + h * RPB_H * RPB_W, [[1, GRID_W], [RPB_W, GRID_H], [1, GRID_W]])
                        dst = bias_rev[p0:p0 + GRID_W, r // 2, SEQ * h:SEQ * h + SEQ]
                        sp.dma_start(dst.rearrange("p (r c) -> p r c", r=GRID_H), src).then_inc(ld_att, 16)
                linear(L["out"], a["w_out_2"][l])
                ffn(2)
            sp.wait_ge(rows_out.sem, rows_out.at(12 + 4))
            sp.dma_start(out[0].rearrange("(t p) d -> p t d", p=P), o_rows[:, :, :]).then_inc(st_out, 16)
            sp.wait_ge(st_out, 16)

        @block.scalar
        def _(act):
            chain = [0]

            def link(ins):
                chain[0] += 1
                ins.then_inc(act_chain.sem, 1)
                act.wait_ge(act_chain.sem, chain[0])

            def split_hi(u, slot, elems):
                if isinstance(u, int) and u >= N_UNITS:
                    return
                act.wait_ge(raw_full[slot], 32 * (u // 2) + 32 if isinstance(u, int) else u * 16 + (32 - 16 * slot))
                need(act, unit_done, u - 1)
                nc.scalar.copy(w_hi[:, slot, 0:elems], raw[:, slot, 0:elems]).then_inc(hi_done.sem, 1)

            def next_hi(stg, i, j, per=4):
                u = stg["u0"] + per * i + j + 1
                slot = (stg["u0"] + j + 1) % 2
                if isinstance(u, int):
                    if u < N_UNITS:
                        split_hi(u, slot, elems_of[u])
                else:
                    split_hi(u, slot, stg["elems"])

            def ada_load(l, j, quarter):
                slot = quarter % 2
                q = 4 * j + quarter
                need(act, ada_mac, 4 * (q - 1))
                k = 2 * quarter
                wv = a["w_ada_2"][l].rearrange("(k p) n -> p k n", p=P)
                c = bass.ds((j - ADA_CHUNKS * l) * ADA_COLS, ADA_COLS)
                act.dma_start(ada_w[:, slot, :, :], wv[:, k:k + 2, c]).then_inc(ada_full[slot], 16)

            def linear(stg):
                for i in range(stg["units"]):
                    u = stg["u0"] + i
                    if u + 1 < N_UNITS:
                        split_hi(u + 1, (u + 1) % 2, elems_of[u + 1])

            def norm(nm, after, h, T, first=0, scale=None, shift=None, dest=None, splits=((0, None),)):
                n = norm_of[nm]
                need(act, acc_free, after)
                for k in range(KD):
                    if k >= 2:
                        need(act, n["ms"], k - 1)
                    nc.scalar.activation(tmp_b[:, k % 2, 0:T], h[:, k, first:first + T], ACT.Square).then_inc(n["sq"].sem, 1)
                need(act, n["ms"], KD)
                nc.scalar.activation(rstd[:, 0:T], ps[:, 5, 0:T], ACT.Sqrt, bias=eps).then_inc(n["root"].sem, 1)
                for k in range(KD):
                    need(act, n["t"], k + 1)
                    if dest is None and k >= 2:
                        need(act, n["lo"], k - 1)
                    o = tmp_b[:, k % 2, :] if dest is None else dest[:, k, :]
                    for q, (c0, c1) in enumerate(splits):
                        ins = nc.scalar.activation(o[:, c0:c1], tmp_a[:, k % 2, c0:c1], ACT.Identity, scale=scale(k, q),
                                                   bias=shift(k, q) if shift else 0.0)
                    ins.then_inc(n["w"].sem, 1)

            def ffn_up(stg, sig, T, n_units, hi, l, ada):
                first, per = ADA[ada] if ada else (0, 0)
                plan = ada_plan(per)

                def step(i, j, work):
                    next_hi(stg, i, j)
                    if work:
                        for c, quarter in plan[j][0]:
                            ada_load(l, first + per * i + c, quarter)
                    n = 4 * i + j
                    g = stg["g0"] + j
                    act.wait_ge(unit_done.sem, stg["u0"] + n + 1)
                    need(act, acc_free, stg["g0"] + n - 1)
                    nc.scalar.activation(tmp_a[:, j % 2, 0:T], ps[:, 2 * (g % 2), 0:T], ACT.Silu).then_inc(sig["silu"].sem, 1)
                    act.wait_ge(acc_free.sem, stg["g0"] + n + 1)
                    row = hi[:, n, 0:T] if isinstance(n, int) else hi[:, bass.ds(n, 1), 0:T].rearrange("p o t -> p (o t)")
                    nc.scalar.copy(row, tmp_b[:, j % 2, 0:T]).then_inc(sig["hi"].sem, 1)

                def body(i):
                    for j in range(4):
                        step(i, j, True)
                repeat(act, n_units // 4, body)
                for j in range(n_units % 4):
                    step(n_units // 4, j, False)

            def ffn_down(stg, l, ada):
                first, per = ADA[ada] if ada else (0, 0)
                plan = ada_plan(per)

                def body(i):
                    for j in range(4):
                        next_hi(stg, i, j)
                        for c, quarter in plan[j][0]:
                            ada_load(l, first + per * i + c, quarter)
                repeat(act, 4, body)

            act.wait_ge(ld_rows, 16 * N_ROWS)
            split_hi(0, 0, UNIT)
            need(act, rows_out, 1)
            nc.scalar.activation(sc_c[:, :, 0], vec[:, 0:8], ACT.Silu)
            nc.scalar.activation(sc_c[:, :, 1], vec[:, 8:16], ACT.Silu).then_inc(act_chain.sem, 1)
            chain[0] += 1

            need(act, rows_out, 5)
            norm("mix1", 0, h1, T1, scale=lambda k, q: vec[:, VEC["norm_mix"][0] + k:VEC["norm_mix"][0] + k + 1],
                 splits=((0, T1),))
            linear(st_in1)

            done(act, "z_sum")
            bg = VEC["b_gate"][0]
            for t in range(2):
                ins = nc.scalar.activation(lga[:, t, :], ps[:, 4 + t, 0:T1], ACT.Abs, bias=vec[:, bg + t:bg + t + 1])
            link(ins)
            link(nc.scalar.activation(lga[:, :, :], lga[:, :, :], ACT.Exp, scale=-1.0))
            nc.scalar.activation(lga[:, :, :], lga[:, :, :], ACT.Ln, bias=one).then_inc(ev["z_ln"], 1)
            done(act, "b_sum")
            nc.scalar.activation(lga[:, :, :], lgb[:, :, :], ACT.Exp)
            nc.scalar.activation(kt[:, :, :], lgb[:, :, :], ACT.Exp, scale=-1.0)
            for t in range(2):
                for c0, n in CHUNKS:
                    ins = nc.scalar.activation(kend[:, t, c0:c0 + n], lgb[:, t, c0:c0 + n], ACT.Exp, scale=-1.0,
                                               bias=lgb[:, t, c0 + n - 1:c0 + n])
            ins.then_inc(ev["exps"], 1)
            for n in range(5):
                done(act, "chunk_turned", n + 1)
                L = CHUNKS[n][1]
                nc.scalar.copy(v_tok[0:L, n, :], ps[0:L, 0 + 2 * (n % 2), :])
                nc.scalar.copy(k_tok[0:L, n, :], ps[0:L, 1 + 2 * (n % 2), 0:256]).then_inc(ev["chunk_rows"], 1)
            nc.scalar.activation(proj1[:, 12:16, :], proj1[:, 12:16, :], ACT.Silu).then_inc(ev["silu_r"], 1)
            done(act, "o_out", 5)
            nc.scalar.activation(proj1[:, 0:4, :], oT[:, :, :], ACT.Square).then_inc(ev["o_sq"], 1)
            done(act, "o_ms")
            nc.scalar.activation(proj1[:, 4:8, :], ps[:, 0:4, 0:T1], ACT.Sqrt, scale=float(D // P), bias=eps).then_inc(ev["o_root"], 1)
            linear(st_out1)
            norm("ffn1", end_of(st_out1), h1, T1, scale=lambda k, q: vec[:, VEC["norm_ffn"][0] + k:VEC["norm_ffn"][0] + k + 1],
                 splits=((0, T1),))
            done(act, "g_shift")
            nc.scalar.activation(r4b[:, :, :], r4a[:, :, :], ACT.Exp).then_inc(ev["g_exp"], 1)
            done(act, "e_shift")
            nc.scalar.activation(prob[:, :, :], r4c[:, :, :], ACT.Exp).then_inc(ev["e_exp"], 1)
            for e in range(N_EXPERTS):
                done(act, "share_sum", e + 1)
                nc.scalar.copy(comb[:, e, :], ps[:, 4 + e % 4, 0:T1]).then_inc(ev["share_out"], 1)
            ffn_up(st_moe_a, moe_sig, T1, MOE_F, hm_hi, 0, None)
            ffn_down(st_moe_b, 0, "moe_b")
            fin = VEC["final"][0]
            norm("end1", end_of(st_moe_b), h1, SEQ, first=N_META, scale=lambda k, q: vec[:, fin + k:fin + k + 1], dest=h2, splits=((0, SEQ),))
            both = ((0, SEQ), (SEQ, T2))

            def modulated(nm, after, l, m, T):
                t0 = 72 * l + 8 * m
                norm(nm, end_of(after), h2, T, scale=lambda k, q: coef[:, k, q:q + 1], shift=lambda k, q: mod[:, t0 + k, q:q + 1],
                     splits=both if T == T2 else both[:1])

            for l in range(2):
                L, A = layers[l], attn[l]
                last = l == 1
                TQ = SEQ if last else T2
                modulated(f"l{l}a", layers[0]["f2b"] if last else st_moe_b, l, 0, T2)
                ffn_up(L["f1a"], L["sig"][0], T2, FFN_F, hf_hi, 0, None if last else "f1a")
                ffn_down(L["f1b"], 0, None if last else "f1b")
                modulated(f"l{l}b", L["f1b"], l, 3, T2)
                linear(L["q"])
                linear(L["kv"])

                for i, t in enumerate(NORM_TILES):
                    Tn = T2 if t == KB else TQ
                    act.wait_ge(acc_free.sem, L["kv"]["g0"] + 5)
                    if i >= 1:
                        need(act, A["pre_dve"], 2 * i)
                    nc.scalar.activation(tmp_b[:, 0, 0:Tn], proj2[:, t, 0:Tn], ACT.Square).then_inc(A["pre_act"].sem, 1)
                    need(act, A["pre_pe"], i + 1)
                    nc.scalar.activation(tmp_b[:, 1, 0:Tn], ps[:, 4, 0:Tn], ACT.Sqrt, bias=eps).then_inc(A["pre_act"].sem, 1)
                for i in range(5):
                    need(act, A["pre_pe"], 3 + i + 1)
                    nc.scalar.copy(vt[:, i, :, :], ps[:, 6 + i % 2, :].rearrange("p (t d) -> p t d", t=4)).then_inc(A["pre_act"].sem, 1)
                need(act, A["pre_dve"], 6 + 21)
                for w, t in ((0, KA), (1, KB)):
                    nc.scalar.copy(k_sw[0:HD, w, :], proj2[HD:P, t, :])
                    ins = nc.scalar.copy(k_sw[HD:P, w, :], proj2[0:HD, t, :])
                ins.then_inc(A["pre_act"].sem, 1)

                def exps(i):
                    n, q0, k0, nk = A["items"][i]
                    x = i % 2
                    need(act, A["logits"], i + 1)
                    for q in range(2):
                        src = s[:, x, q, 0:nk] if kind(n) != "B" and q0 == 0 else scores_of(i)[:, q, :]
                        scale = 1.0 if kind(n) != "B" and q0 == 0 else HD ** -0.5
                        ins = nc.scalar.activation(s[:, x, q, 0:nk], src, ACT.Exp, scale=scale,
                                                   bias=st[:, x, q:q + 1], accum_out=st[:, x, 2 + q:3 + q])
                    if kind(n) == "A":
                        ins = nc.scalar.activation(st[:, x, 4:6], st[:, x, 0:2], ACT.Exp, bias=sink[:, n:n + 1])
                    ins.then_inc(A["exped"].sem, 1)

                def outs(i):
                    n, q0, k0, nk = A["items"][i]
                    x = i % 2
                    need(act, A["turned"], i + 1)
                    kts = nk // P
                    nc.scalar.copy(pT[:, x, 0:kts, :], ps[:, 4:6, :].rearrange("p b (t q) -> p (b t) q", t=2)[:, 0:kts, :]).then_inc(A["pt"].sem, 1)

                def yhi(i):
                    n, q0, k0, nk = A["items"][i]
                    off = HD * (n % 2)
                    need(act, A["o"], i + 1)
                    nc.scalar.copy(u_hi[off:off + HD, n // 2, q0:q0 + 256], ps[off:off + HD, 6 + i % 2, 0:256]).then_inc(A["yhi"].sem, 1)

                def scores_of(i):
                    nk = A["items"][i][3]
                    return ps[:, 2 * (i % 2):2 * (i % 2) + 2, 0:nk]

                N = len(A["items"])
                for i in range(N + 2):
                    if i < N:
                        exps(i)
                    if 1 <= i <= N:
                        outs(i - 1)
                    if i >= 2:
                        yhi(i - 2)
                linear(L["out"])
                modulated(f"l{l}c", L["out"], l, 6, TQ)
                ffn_up(L["f2a"], L["sig"][1], TQ, FFN_F, hf_hi, 1, None if last else "f2a")
                ffn_down(L["f2b"], 1, None if last else "f2b")
            fin = VEC["final2"][0]
            norm("end2", end_of(layers[1]["f2b"]), h2, SEQ, scale=lambda k, q: vec[:, fin + k:fin + k + 1], dest=h2, splits=((0, SEQ),))

        @block.vector
        def _(dve):
            chain = [0]

            def link(ins):
                chain[0] += 1
                ins.then_inc(dve_chain.sem, 1)
                dve.wait_ge(dve_chain.sem, chain[0])

            tt, ts, stt = nc.vector.tensor_tensor, nc.vector.tensor_scalar, nc.vector.scalar_tensor_tensor

            def split_lo(u, slot, elems):
                dve.wait_ge(hi_done.sem, u + 1)
                tt(w_lo[:, slot, 0:elems], raw[:, slot, 0:elems], w_hi[:, slot, 0:elems].bitcast(F32),
                   ALU.subtract).then_inc(lo_done.sem, 1)

            def next_lo(stg, i, j, per=4):
                u = stg["u0"] + per * i + j + 1
                slot = (stg["u0"] + j + 1) % 2
                if isinstance(u, int):
                    if u < N_UNITS:
                        split_lo(u, slot, elems_of[u])
                else:
                    split_lo(u, slot, stg["elems"])

            def ada_quarter(j, quarter):
                slot = quarter % 2
                dve.wait_ge(ada_full[slot], 32 * j + 16 * (quarter // 2) + 16)
                for kk in range(2):
                    k = 2 * quarter + kk
                    for v in range(2):
                        if k == 0:
                            if v == 0:
                                need(dve, ada_sum, j)
                            ins = ts(ada_acc[:, v, :], ada_w[:, slot, kk, :], sc_c[:, k, v:v + 1], None, ALU.mult)
                        else:
                            dve.wait_ge(ada_mac.sem, 16 * j + 2 * k + v - 1)
                            ins = stt(out=ada_acc[:, v, :], in0=ada_w[:, slot, kk, :], scalar=sc_c[:, k, v:v + 1],
                                      in1=ada_acc[:, v, :], op0=ALU.mult, op1=ALU.add)
                        ins.then_inc(ada_mac.sem, 1)

            def ada_out(j):
                dve.wait_ge(ada_sum.sem, j + 1)
                nj = ADA_COLS // P
                v = bass.ds(nj * j, nj)
                tt(mod[:, v, :], ps[:, 4, 0:2 * nj].rearrange("p (t v) -> p t v", v=2), b_ada[:, v, :],
                   ALU.add).then_inc(mod_done.sem, 1)

            def norm(nm, h, T, first=0, split=True):
                n = norm_of[nm]
                need(dve, n["root"], 1)
                nc.vector.reciprocal(rstd[:, 0:T], rstd[:, 0:T]).then_inc(n["rstd"].sem, 1)
                need(dve, n["rstd"], 1)

                def t_row(k):
                    if k >= 2:
                        need(dve, n["w"], k - 1)
                    tt(tmp_a[:, k % 2, 0:T], h[:, k, first:first + T], rstd[:, 0:T], ALU.mult).then_inc(n["t"].sem, 1)

                t_row(0)
                for k in range(KD):
                    if k + 1 < KD:
                        t_row(k + 1)
                    if split:
                        need(dve, n["w"], k + 1)
                        nc.vector.tensor_copy(u_hi[:, k, 0:T], tmp_b[:, k % 2, 0:T]).then_inc(n["hi"].sem, 1)

            def ffn_up(stg, sig, T, n_units, ada, weighted=False):
                first, per = ADA[ada] if ada else (0, 0)
                plan = ada_plan(per)

                def step(i, j, work):
                    next_lo(stg, i, j)
                    n = 4 * i + j
                    g = stg["g0"] + j
                    if work and plan[j][1] is not None:
                        c = first + per * i + plan[j][1]
                        if not (isinstance(c, int) and c < first):
                            ada_out(c)
                    need(dve, sig["silu"], n + 1)
                    if weighted:
                        e = 2 * i + j // 2
                        ce = comb[:, e, :] if isinstance(e, int) else comb[:, bass.ds(e, 1), :].rearrange("p o t -> p (o t)")
                        tt(tmp_a[:, j % 2, 0:T], tmp_a[:, j % 2, 0:T], ce, ALU.mult).then_inc(sig["comb"].sem, 1)
                        need(dve, sig["comb"], n + 1)
                    need(dve, sig["lo"], n - 1)
                    tt(tmp_b[:, j % 2, 0:T], tmp_a[:, j % 2, 0:T], ps[:, 2 * (g % 2) + 1, 0:T], ALU.mult).then_inc(acc_free.sem, 1)
                    if work:
                        for c, quarter in plan[j][0]:
                            ada_quarter(first + per * i + c, quarter)

                def body(i):
                    for j in range(4):
                        step(i, j, True)
                nb = n_units // 4
                repeat(dve, nb, body)
                if ada and n_units % 4 == 0:
                    ada_out(first + per * nb - 1)
                for j in range(n_units % 4):
                    step(nb, j, False)
                    if j == 0 and ada:
                        ada_out(first + per * nb - 1)

            def ffn_down(stg, add, ada):
                first, per = ADA[ada] if ada else (0, 0)
                plan = ada_plan(per)

                def body(i):
                    for j in range(4):
                        next_lo(stg, i, j)
                        if plan[j][1] is not None:
                            c = first + per * i + plan[j][1]
                            if not (isinstance(c, int) and c < first):
                                ada_out(c)
                        if j % 2:
                            m = 2 * i + j // 2
                            dve.wait_ge(unit_done.sem, stg["u0"] + 4 * i + j + 1)
                            add(m, ps[:, 2 * ((stg["g0"] + j // 2) % 2), :]).then_inc(acc_free.sem, 1)
                        for c, quarter in plan[j][0]:
                            ada_quarter(first + per * i + c, quarter)
                repeat(dve, 4, body)
                if ada:
                    ada_out(first + per * 4 - 1)

            def row(h, m, c0, c1):
                return h[:, m, c0:c1] if isinstance(m, int) else h[:, bass.ds(m, 1), c0:c1].rearrange("p o t -> p (o t)")

            def add_plain(m, acc):
                return tt(row(h1, m, 0, T1), acc[:, 0:T1], row(h1, m, 0, T1), ALU.add)

            def add_gated(T):
                def add(m, acc):
                    for v in range(T // SEQ):
                        c0 = SEQ * v
                        g = gate[:, m, v:v + 1] if isinstance(m, int) else gate[:, bass.ds(m, 1), v:v + 1].rearrange("p o t -> p (o t)")
                        ins = stt(out=row(h2, m, c0, c0 + SEQ), in0=acc[:, c0:c0 + SEQ], scalar=g,
                                  in1=row(h2, m, c0, c0 + SEQ), op0=ALU.mult, op1=ALU.add)
                    return ins
                return add

            def linear(stg, take):
                for i in range(stg["units"]):
                    u, g = stg["u0"] + i, stg["g0"] + i
                    if u + 1 < N_UNITS:
                        split_lo(u + 1, (u + 1) % 2, elems_of[u + 1])
                    dve.wait_ge(unit_done.sem, u + 1)
                    take(i, ps[:, 2 * (g % 2):2 * (g % 2) + 2, :]).then_inc(acc_free.sem, 1)

            need(dve, turned, 1)
            nc.vector.tensor_copy(vec[:, :], ps[:, 0, 0:VEC_ROWS]).then_inc(rows_out.sem, 1)
            need(dve, turned, 2)
            nc.vector.tensor_copy(h1[:, :, 0:N_META], ps[:, 1, 0:128].rearrange("p (k t) -> p k t", k=KD)
                                  ).then_inc(rows_out.sem, 1)
            for b in range(4):
                need(dve, turned, 3 + min(b, 2))
                ins = nc.vector.tensor_copy(h1[:, 2 * b:2 * b + 2, N_META:T1], ps[:, 2 + b, :].rearrange("p (k t) -> p k t", k=2))
                if b != 2:
                    ins.then_inc(rows_out.sem, 1)
            for t in range(4):
                need(dve, turned, 6 + t)
                nc.vector.tensor_copy(h2[:, 2 * t:2 * t + 2, SEQ:T2], ps[:, 6 + t % 2, :].rearrange("p (k t) -> p k t", k=2)).then_inc(rows_out.sem, 1)
            need(dve, turned, 10)
            for v in range(2):
                for l in range(2):
                    ins = nc.vector.tensor_copy(b_ada[:, 72 * l:72 * l + 72, v], ps[:, 0, 72 * l:72 * l + 72])
            ins.then_inc(rows_out.sem, 3)
            split_lo(0, 0, UNIT)
            norm("mix1", h1, T1)

            def to_proj1(i, acc):
                if i == 0:
                    dve.wait_ge(rows_out.sem, rows_out.at(12))
                return nc.vector.tensor_copy(proj1[:, 2 * i:2 * i + 2, :], acc[:, :, 0:T1])
            linear(st_in1, to_proj1)

            dve.wait_ge(ld_small, 64)
            link(nc.vector.tensor_copy(glr_hi[:, :, :], glr_raw[:, :, :]))
            tt(glr_lo[:, :, :], glr_raw[:, :, :], glr_hi[:, :, :].bitcast(F32), ALU.subtract).then_inc(ev["low_split"], 1)
            done(dve, "win_zero")
            link(nc.vector.tensor_copy(win_a[:, :, PAD:PAD + T1], proj1[:, 0:4, :]))
            n = PAD + T1
            link(tt(win_b[:, :, 1:n], win_a[:, :, 1:n], win_a[:, :, 0:n - 1], ALU.add))
            link(tt(win_a[:, 1:4, 3:n], win_b[:, 1:4, 3:n], win_b[:, 1:4, 1:n - 2], ALU.add))
            link(tt(win_b[:, 2:4, 7:n], win_a[:, 2:4, 7:n], win_a[:, 2:4, 3:n - 4], ALU.add))
            link(tt(win_a[:, 3:4, 15:n], win_b[:, 3:4, 15:n], win_b[:, 3:4, 7:n - 8], ALU.add))
            for g, w in enumerate((win_b, win_a, win_b, win_a)):
                ins = tt(w[:, g, PAD:n], w[:, g, PAD:n], cnt[:, g, :], ALU.mult)
            link(ins)
            for g, w in enumerate((win_b, win_a, win_b, win_a)):
                ins = tt(w[:, g, PAD:n], w[:, g, PAD:n], proj1[:, g, :], ALU.subtract)
            ins.then_inc(ev["windows"], 1)
            done(dve, "low_sum")
            nc.vector.tensor_copy(glr[:, :], ps[:, 4, 0:T1]).then_inc(ev["low_out"], 1)
            done(dve, "z_ln")
            bg = VEC["b_gate"][0]
            for t in range(2):
                ins = ts(lgb[:, t, :], ps[:, 4 + t, 0:T1], vec[:, bg + t:bg + t + 1], 0.0, ALU.add, ALU.min)
            link(ins)
            link(tt(lga[:, :, :], lgb[:, :, :], lga[:, :, :], ALU.subtract))
            link(ts(lga[:, :, :], lga[:, :, :], 1.0 / 16.0, None, ALU.mult))
            for t in range(2):
                for c0, L in CHUNKS:
                    ins = nc.vector.tensor_tensor_scan(lgb[:, t, c0:c0 + L], one.to_broadcast([P, L]),
                                                       lga[:, t, c0:c0 + L], 0.0, ALU.mult, ALU.add)
            ins.then_inc(ev["b_sum"], 1)
            done(dve, "exps")
            for h in range(4):
                o, t = HD * (h % 2), h // 2
                stt(out=qz[o:o + HD, h, :], in0=proj1[o:o + HD, 4 + t, :], scalar=HD ** -0.5, in1=lga[o:o + HD, t, :],
                    op0=ALU.mult, op1=ALU.mult)
            tt(kend[:, :, :], kend[:, :, :], proj1[:, 6:8, :], ALU.mult)
            tt(kt[:, :, :], kt[:, :, :], proj1[:, 6:8, :], ALU.mult).then_inc(ev["keys"], 1)
            done(dve, "pooled_sum", 4)
            sc0 = VEC["pool_scale"][0]
            for g in range(4):
                if g:
                    done(dve, "pooled_out", g)
                link(ts(tmp_a[:, 0, 0:T1], ps[:, 4 + g, 0:T1], vec[:, sc0 + g:sc0 + g + 1], None, ALU.mult))
                link(nc.vector.tensor_copy(u_hi[:, g, 0:T1], tmp_a[:, 0, 0:T1]))
                tt(u_lo[:, g, 0:T1], tmp_a[:, 0, 0:T1], u_hi[:, g, 0:T1].bitcast(F32),
                   ALU.subtract).then_inc(ev["pooled_out"], 1)
            for n, (c0, L) in enumerate(CHUNKS):
                done(dve, "scores", n + 1)
                if n >= 2:
                    done(dve, "o_sum", n - 1)
                nc.vector.tensor_copy(sT[0:L, n % 2, :, 0:L],
                                      ps[0:L, 6, 0:256].rearrange("p (h c) -> p h c", h=4)[:, :, 0:L]
                                      ).then_inc(ev["scores_out"], 1)
                done(dve, "o_sum", n + 1)
                nc.vector.tensor_copy(oT[:, :, c0:c0 + L], ps[:, 7, 0:256].rearrange("p (h c) -> p h c", h=4)
                                      [:, :, 0:L]).then_inc(ev["o_out"], 1)
                if n == len(CHUNKS) - 1:
                    break
                done(dve, "chunk_state", n + 1)
                if n:
                    done(dve, "state", n)
                d = ps[:, 4 + n % 2, :].rearrange("p (h v) -> p h v", h=4)
                if n == 0:
                    ins = nc.vector.tensor_copy(S[:, :, :], d)
                else:
                    for h in range(4):
                        ins = stt(out=S[:, h, :], in0=S[:, h, :], scalar=lga[:, h // 2, c0 + L - 1:c0 + L], in1=d[:, h, :],
                                  op0=ALU.mult, op1=ALU.add)
                ins.then_inc(ev["state"], 1)
            done(dve, "o_root")
            done(dve, "silu_r")
            link(nc.vector.reciprocal(proj1[:, 4:8, :], proj1[:, 4:8, :]))
            link(tt(oT[:, :, :], oT[:, :, :], proj1[:, 4:8, :], ALU.mult))
            gw = VEC["gla_norm"][0]
            link(stt(out=oT[:, :, :], in0=oT[:, :, :], scalar=vec[:, gw:gw + 1], in1=proj1[:, 12:16, :], op0=ALU.mult, op1=ALU.mult))
            link(nc.vector.tensor_copy(u_hi[:, 4:8, 0:T1], oT[:, :, :]))
            tt(u_lo[:, 4:8, 0:T1], oT[:, :, :], u_hi[:, 4:8, 0:T1].bitcast(F32), ALU.subtract).then_inc(y_ready[0].sem, 8)

            def add_h1(i, acc):
                return tt(h1[:, 2 * i:2 * i + 2, :], acc[:, :, 0:T1], h1[:, 2 * i:2 * i + 2, :], ALU.add)
            linear(st_out1, add_h1)

            norm("ffn1", h1, T1)
            dve.wait_ge(ld_router, 64)
            link(nc.vector.tensor_copy(wr_hi[:, :, :], wr[:, :, :]))
            tt(wr_lo[:, :, :], wr[:, :, :], wr_hi[:, :, :].bitcast(F32), ALU.subtract).then_inc(ev["r_split"], 1)
            done(dve, "logits")
            for t in range(3):
                ins = tt(lg[:, t, :], ps[:, 6, 20 * t:20 * t + 20], rb[:, :], ALU.add)
            link(ins)

            def spread(v, n=4):
                return v.rearrange("p (t o) -> p t o", o=1).to_broadcast([P, 3, n])

            ranks = rank.rearrange("p (o k) -> p o k", o=1).to_broadcast([P, 3, 4])

            def first_of(dst, v, top, scratch, m):
                link(tt(scratch[:, :, :], v, spread(top), ALU.is_equal))
                link(tt(scratch[:, :, :], scratch[:, :, :], ranks, ALU.mult))
                link(nc.vector.reduce_max(m[:, :], scratch[:, :, :], AX_X))
                link(tt(dst, scratch[:, :, :], spread(m[:, :]), ALU.is_equal))

            link(nc.vector.reduce_max(r1a[:, :], lg[:, :, 0:4], AX_X))
            tt(r4a[:, :, :], lg[:, :, 0:4], spread(r1a[:, :]), ALU.subtract).then_inc(ev["g_shift"], 1)
            first_of(oh_g[:, :, :], lg[:, :, 0:4], r1a[:, :], r4c, r1b)
            link(tt(r16[:, :, :].rearrange("p t (g k) -> p t g k", g=4), lg[:, :, 4:20].rearrange("p t (g k) -> p t g k", g=4),
                    oh_g[:, :, :].rearrange("p t (g o) -> p t g o", o=1).to_broadcast([P, 3, 4, 4]), ALU.mult))
            link(nc.vector.reduce_sum(r4c[:, :, :], r16[:, :, :].rearrange("p t (g k) -> p t k g", g=4), AX_X))
            link(nc.vector.reduce_max(r1b[:, :], r4c[:, :, :], AX_X))
            tt(r4c[:, :, :], r4c[:, :, :], spread(r1b[:, :]), ALU.subtract).then_inc(ev["e_shift"], 1)
            done(dve, "g_exp")
            link(nc.vector.reduce_sum(pg[:, :], r4b[:, :, :], AX_X))
            link(nc.vector.reciprocal(pg[:, :], pg[:, :]))
            done(dve, "e_exp")
            link(nc.vector.reduce_sum(r1a[:, :], prob[:, :, :], AX_X))
            link(nc.vector.reciprocal(r1a[:, :], r1a[:, :]))
            link(tt(prob[:, :, :], prob[:, :, :], spread(r1a[:, :]), ALU.mult))
            link(nc.vector.reduce_max(r1a[:, :], prob[:, :, :], AX_X))
            first_of(oh1[:, :, :], prob[:, :, :], r1a[:, :], r4c, r1b)
            link(stt(out=r4b[:, :, :], in0=oh1[:, :, :], scalar=-2.0, in1=prob[:, :, :], op0=ALU.mult, op1=ALU.add))
            link(nc.vector.reduce_max(r1c[:, :], r4b[:, :, :], AX_X))
            first_of(r4a[:, :, :], r4b[:, :, :], r1c[:, :], r4c, r1b)
            link(tt(r4a[:, :, :], r4a[:, :, :], oh1[:, :, :], ALU.add))
            link(tt(r1a[:, :], r1a[:, :], r1c[:, :], ALU.add))
            link(nc.vector.reciprocal(r1a[:, :], r1a[:, :]))
            link(tt(r1a[:, :], r1a[:, :], pg[:, :], ALU.mult))
            link(tt(r4a[:, :, :], r4a[:, :, :], prob[:, :, :], ALU.mult))
            link(tt(r4a[:, :, :], r4a[:, :, :], spread(r1a[:, :]), ALU.mult))
            for t in range(3):
                ins = tt(r16[:, t, :].rearrange("p (g k) -> p g k", g=4),
                         oh_g[:, t, :].rearrange("p (g o) -> p g o", o=1).to_broadcast([P, 4, 4]),
                         r4a[:, t, :].rearrange("p (o k) -> p o k", o=1).to_broadcast([P, 4, 4]), ALU.mult)
            ins.then_inc(ev["shares"], 1)
            done(dve, "shares_turned")
            nc.vector.tensor_copy(combT[:, 0:256], ps[0:16, 7, 0:256])
            nc.vector.tensor_copy(combT[:, 256:272], ps[0:16, 7, 256 + 112:384]).then_inc(ev["shares_out"], 1)
            ffn_up(st_moe_a, moe_sig, T1, MOE_F, None, weighted=True)
            ffn_down(st_moe_b, add_plain, "moe_b")
            norm("end1", h1, SEQ, first=N_META, split=False)
            def modulation(l, nw, m, after):
                t0 = 72 * l + 8 * m
                w0 = VEC[nw][0] + 8 * l
                need(dve, acc_free, end_of(after))
                need(dve, mod_done, 36 if l else {0: 4, 3: 14, 6: 18}[m])
                for v in range(2):
                    ins = stt(out=coef[:, :, v], in0=mod[:, t0 + 8:t0 + 16, v], scalar=1.0, in1=vec[:, w0:w0 + 8],
                              op0=ALU.add, op1=ALU.mult)
                link(ins)

            def gates(l, m, by):
                t0 = 72 * l + 8 * m + 16
                need(dve, mod_done, 36 if l else {0: 14, 3: 14, 6: 18}[m])
                link(ts(gate[:, :, :], mod[:, t0:t0 + 8, :], by, None, ALU.mult))

            for l in range(2):
                L, A = layers[l], attn[l]
                last = l == 1
                TQ = SEQ if last else T2
                modulation(l, "ffn1", 0, layers[0]["f2b"] if last else st_moe_b)
                norm(f"l{l}a", h2, T2)
                ffn_up(L["f1a"], L["sig"][0], T2, FFN_F, None if last else "f1a")
                gates(l, 0, 0.5)
                ffn_down(L["f1b"], add_gated(T2), None if last else "f1b")
                modulation(l, "mix", 3, L["f1b"])
                norm(f"l{l}b", h2, T2)
                gates(l, 3, 1.0)
                linear(L["q"], lambda i, acc: nc.vector.tensor_copy(proj2[:, 2 * i:2 * i + 2, 0:TQ], acc[:, :, 0:TQ]))
                linear(L["kv"], lambda i, acc: nc.vector.tensor_copy(proj2[:, 8 + 2 * i:10 + 2 * i, :], acc))

                for i, t in enumerate(NORM_TILES):
                    Tn = T2 if t == KB else TQ
                    need(dve, A["pre_act"], 2 * i + 2)
                    nc.vector.reciprocal(tmp_b[:, 1, 0:Tn], tmp_b[:, 1, 0:Tn]).then_inc(A["pre_dve"].sem, 1)
                    need(dve, A["pre_dve"], 2 * i + 1)
                    w0 = VEC["k_norm" if t == KB else "q_norm"][0] + l
                    stt(out=proj2[:, t, 0:Tn], in0=proj2[:, t, 0:Tn], scalar=vec[:, w0:w0 + 1], in1=tmp_b[:, 1, 0:Tn],
                        op0=ALU.mult, op1=ALU.mult).then_inc(A["pre_dve"].sem, 1)
                dve.wait_ge(ld_att, (l + 1) * 16 * (2 + GRID_H * C_HEADS))
                for i in range(6):
                    need(dve, A["bias"], i + 1)
                    tt(bias_c[:, i // 3, 2 * (i % 3):2 * (i % 3) + 2, :],
                       ps[:, BIAS_BANKS[i], :].rearrange("p (h k) -> p h k", h=2),
                       nbr_mask.rearrange("p (o k) -> p o k", o=1).to_broadcast([P, 2, SEQ]),
                       ALU.add).then_inc(A["bias_out"].sem, 1)
                need(dve, A["bias_out"], 6)
                for i, t in enumerate(ROPE_TILES):
                    need(dve, A["pre_pe"], 8 + i + 1)
                    b = 6 + i % 2
                    tt(tmp_a[:, 0, 0:SEQ], proj2[:, t, 0:SEQ], cos, ALU.mult).then_inc(A["pre_dve"].sem, 1)
                    tt(tmp_a[:, 1, 0:SEQ], ps[:, b, 0:SEQ], sin, ALU.mult).then_inc(A["pre_dve"].sem, 1)
                    need(dve, A["pre_dve"], 6 + 3 * i + 2)
                    tt(proj2[:, t, 0:SEQ], tmp_a[:, 0, 0:SEQ], tmp_a[:, 1, 0:SEQ], ALU.add).then_inc(A["pre_dve"].sem, 1)
                    need(dve, A["pre_dve"], 6 + 3 * i + 3)
                def scores_of(i):
                    nk = A["items"][i][3]
                    return ps[:, 2 * (i % 2):2 * (i % 2) + 2, 0:nk]

                def logits(i):
                    n, q0, k0, nk = A["items"][i]
                    x = i % 2
                    need(dve, A["scores"], i + 1)
                    if i >= 2:
                        need(dve, A["turned"], i - 1)
                    sc = scores_of(i)
                    c = HD ** -0.5
                    masked = kind(n) != "B" and q0 == 0
                    if kind(n) == "A" and q0 == 0:
                        link(stt(out=s[:, x, :, :], in0=sc, scalar=c, in1=win_mask, op0=ALU.mult, op1=ALU.add))
                    elif kind(n) == "C" and q0 == 0:
                        stt(out=s[:, x, :, 0:SEQ], in0=sc[:, :, 0:SEQ], scalar=c,
                            in1=bias_c[:, :, n - A_HEADS - B_HEADS, :], op0=ALU.mult, op1=ALU.add)
                        link(ts(s[:, x, :, SEQ:T2], sc[:, :, SEQ:T2], c, None, ALU.mult))
                    src = s[:, x, :, :] if masked else sc
                    link(nc.vector.reduce_max(st[:, x, 0:2], src, AX_X))
                    if kind(n) == "A":
                        link(ts(st[:, x, 0:2], st[:, x, 0:2], 1.0 if masked else c, sink[:, n:n + 1], ALU.mult, ALU.max))
                        ts(st[:, x, 0:2], st[:, x, 0:2], -1.0, None, ALU.mult).then_inc(A["logits"].sem, 1)
                    else:
                        ts(st[:, x, 0:2], st[:, x, 0:2], -1.0 if masked else -c, None, ALU.mult).then_inc(A["logits"].sem, 1)

                def normal(i):
                    n, q0, k0, nk = A["items"][i]
                    x = i % 2
                    need(dve, A["exped"], i + 1)
                    if kind(n) == "A":
                        link(tt(st[:, x, 2:4], st[:, x, 2:4], st[:, x, 4:6], ALU.add))
                    link(nc.vector.reciprocal(st[:, x, 6:8], st[:, x, 2:4]))
                    for q in range(2):
                        ins = ts(s[:, x, q, 0:nk], s[:, x, q, 0:nk], st[:, x, 6 + q:7 + q], None, ALU.mult)
                    ins.then_inc(A["probs"].sem, 1)

                def ylo(i):
                    n, q0, k0, nk = A["items"][i]
                    off = HD * (n % 2)
                    need(dve, A["yhi"], i + 1)
                    tt(u_lo[off:off + HD, n // 2, q0:q0 + 256], ps[off:off + HD, 6 + i % 2, 0:256],
                       u_hi[off:off + HD, n // 2, q0:q0 + 256].bitcast(F32), ALU.subtract).then_inc(A["ylo"].sem, 1)

                N = len(A["items"])
                logits(0)
                for i in range(N + 2):
                    if i < N:
                        normal(i)
                    if i + 1 < N:
                        logits(i + 1)
                    if i >= 2:
                        ylo(i - 2)

                def add_h2(i, acc):
                    for t in range(2):
                        for v in range(TQ // SEQ):
                            m, c0 = 2 * i + t, SEQ * v
                            ins = stt(out=h2[:, m, c0:c0 + SEQ], in0=acc[:, t, c0:c0 + SEQ], scalar=gate[:, m, v:v + 1],
                                      in1=h2[:, m, c0:c0 + SEQ], op0=ALU.mult, op1=ALU.add)
                    return ins
                linear(L["out"], add_h2)
                modulation(l, "ffn2", 6, L["out"])
                norm(f"l{l}c", h2, TQ)
                ffn_up(L["f2a"], L["sig"][1], TQ, FFN_F, None if last else "f2a")
                gates(l, 6, 0.5)
                ffn_down(L["f2b"], add_gated(TQ), None if last else "f2b")
            norm("end2", h2, SEQ, split=False)
            for t in range(4):
                dve.wait_ge(turned.sem, turned.at(10 + t + 1))
                nc.vector.tensor_copy(o_rows[:, t // 2, 512 * (t % 2):512 * (t % 2) + 512], ps[:, 2 + t, :]).then_inc(rows_out.sem, 1)

        @block.gpsimd
        def _(pool):
            chain = [0]

            def link(ins):
                chain[0] += 1
                ins.then_inc(pool_chain.sem, 1)
                pool.wait_ge(pool_chain.sem, chain[0])

            tt = nc.gpsimd.tensor_tensor

            def norm(nm, T):
                n = norm_of[nm]
                for k in range(KD):
                    need(pool, n["hi"], k + 1)
                    tt(u_lo[:, k, 0:T], tmp_b[:, k % 2, 0:T], u_hi[:, k, 0:T].bitcast(F32), ALU.subtract).then_inc(n["lo"].sem, 1)

            def ffn_up(sig, T, n_units, hi, lo):
                def step(i, j):
                    n = 4 * i + j
                    need(pool, sig["hi"], n + 1)
                    r = [x[:, n, 0:T] if isinstance(n, int) else x[:, bass.ds(n, 1), 0:T].rearrange("p o t -> p (o t)") for x in (hi, lo)]
                    tt(r[1], tmp_b[:, j % 2, 0:T], r[0].bitcast(F32), ALU.subtract).then_inc(sig["lo"].sem, 1)

                def body(i):
                    for j in range(4):
                        step(i, j)
                repeat(pool, n_units // 4, body)
                for j in range(n_units % 4):
                    step(n_units // 4, j)

            pool.wait_ge(rows_out.sem, rows_out.at(12))
            nc.gpsimd.memset(glr_raw[:, :, :], 0.0).then_inc(ev["low_zero"], 1)
            nc.gpsimd.memset(qz[:, :, :], 0.0)
            norm("mix1", T1)
            nc.gpsimd.memset(win_a[:, :, 0:PAD], 0.0).then_inc(ev["win_zero"], 1)
            for n, (c0, L) in enumerate(CHUNKS):
                done(pool, "scores_out", n + 1)
                nc.gpsimd.affine_select(out=sT[0:L, n % 2, :, 0:L], in_=sT[0:L, n % 2, :, 0:L], compare_op=ALU.is_ge, fill=0.0,
                                        base=0, pattern=[[0, 4], [1, L]], channel_multiplier=-1).then_inc(ev["causal"], 1)
            norm("ffn1", T1)
            ffn_up(moe_sig, T1, MOE_F, hm_hi, hm_lo)
            for l in range(2):
                TQ = SEQ if l == 1 else T2
                norm(f"l{l}a", T2)
                ffn_up(layers[l]["sig"][0], T2, FFN_F, hf_hi, hf_lo)
                norm(f"l{l}b", T2)
                norm(f"l{l}c", TQ)
                ffn_up(layers[l]["sig"][1], TQ, FFN_F, hf_hi, hf_lo)

        @block.tensor
        def _(pe):
            mm = nc.tensor.matmul

            def turn(dst, src, n):
                return nc.tensor.transpose(dst, src, ident[0:n, 0:n])

            def products(acc, slot, cols, moving, T, first, last):
                n = len(moving)
                for i, (c, (m_hi, m_lo)) in enumerate(zip(cols, moving)):
                    w1, w2 = w_hi[:, slot, c:c + P], w_lo[:, slot, c:c + P]
                    mm(acc, w1, m_hi, start=(first and i == 0), stop=False)
                    mm(acc, w1, m_lo, start=False, stop=False)
                    ins = mm(acc, w2, m_hi, start=False, stop=(last and i == n - 1))
                return ins

            def rows_of(hi, lo, k0, n, T):
                return [(hi[:, k, 0:T], lo[:, k, 0:T]) for k in range(k0, k0 + n)]

            def begin(u, g):
                pe.wait_ge(lo_done.sem, u + 1)
                if g is not None:
                    need(pe, acc_free, g - 1)

            def norm(nm, T):
                n = norm_of[nm]
                for k in range(KD):
                    need(pe, n["sq"], k + 1)
                    mm(ps[:, 5, 0:T], ones_d, tmp_b[:, k % 2, 0:T], start=(k == 0), stop=(k == KD - 1)).then_inc(n["ms"].sem, 1)

            def linear(stg, T, ready):
                for i in range(stg["units"]):
                    u, g = stg["u0"] + i, stg["g0"] + i
                    begin(u, g)
                    if i == 0:
                        pe.wait_ge(ready.sem, ready.at(8))
                    for t in range(2):
                        ins = products(ps[:, 2 * (g % 2) + t, 0:T], u % 2, [2 * P * k + P * t for k in range(KD)],
                                       rows_of(u_hi, u_lo, 0, KD, T), T, True, True)
                    ins.then_inc(unit_done.sem, 1)

            def ada_sums(j):
                pe.wait_ge(ada_mac.sem, 16 * j + 16)
                need(pe, mod_done, j)
                for t in range(ADA_COLS // P):
                    for v in range(2):
                        ins = mm(ps[:, 4, 2 * t + v:2 * t + v + 1], ada_acc[:, v, P * t:P * t + P], one, start=True, stop=True)
                ins.then_inc(ada_sum.sem, 1)

            def ffn_up(stg, T, n_units, ready, ada):
                first, per = ADA[ada] if ada else (0, 0)
                plan = ada_plan(per)

                def step(i, j, work):
                    begin(stg["u0"] + 4 * i + j, stg["g0"] + 4 * i + j)
                    if isinstance(i, int) and i == 0 and j == 0:
                        pe.wait_ge(ready.sem, ready.at(8))
                    g, slot = (stg["g0"] + j) % 2, (stg["u0"] + j) % 2
                    for t in range(2):
                        ins = products(ps[:, 2 * g + t, 0:T], slot, [8 * P * t + P * k for k in range(KD)],
                                       rows_of(u_hi, u_lo, 0, KD, T), T, True, True)
                    ins.then_inc(unit_done.sem, 1)
                    if work and plan[j][1] is not None:
                        c = first + per * i + plan[j][1]
                        if not (isinstance(c, int) and c < first):
                            ada_sums(c)

                def body(i):
                    for j in range(4):
                        step(i, j, True)
                nb = n_units // 4
                repeat(pe, nb, body)
                if ada and n_units % 4 == 0:
                    ada_sums(first + per * nb - 1)
                for j in range(n_units % 4):
                    step(nb, j, False)
                    if j == 0 and ada:
                        ada_sums(first + per * nb - 1)

            def ffn_down(stg, sig, T, kt2, hi, lo, n_hidden, ada):
                first, per = ADA[ada] if ada else (0, 0)
                plan = ada_plan(per)

                def body(i):
                    for j in range(4):
                        begin(stg["u0"] + 4 * i + j, stg["g0"] + 2 * i + j // 2 if j % 2 == 0 else None)
                        if isinstance(i, int) and i == 0 and j < 2:
                            need(pe, sig["lo"], kt2 * (j + 1))
                        g, slot = (stg["g0"] + j // 2) % 2, (stg["u0"] + j) % 2
                        products(ps[:, 2 * g, 0:T], slot, [P * k for k in range(kt2)],
                                 rows_of(hi, lo, kt2 * (j % 2), kt2, T), T, j % 2 == 0, j % 2 == 1).then_inc(unit_done.sem, 1)
                        if plan[j][1] is not None:
                            c = first + per * i + plan[j][1]
                            if not (isinstance(c, int) and c < first):
                                ada_sums(c)
                repeat(pe, 4, body)
                if ada:
                    ada_sums(first + per * 4 - 1)

            pe.wait_ge(ld_rows, 16 * N_ROWS)
            turn(ps[:, 0, 0:VEC_ROWS], vec_rows[:, :], VEC_ROWS).then_inc(turned.sem, 1)
            pe.wait_ge(ld_x, 48)
            for k in range(KD):
                ins = turn(ps[:, 1, 16 * k:16 * k + 16], meta_rows[:, P * k:P * k + P], N_META)
            ins.then_inc(turned.sem, 1)
            for b in range(4):
                for k in (2 * b, 2 * b + 1):
                    for t in range(2):
                        ins = turn(ps[:, 2 + b, 256 * (k % 2) + P * t:256 * (k % 2) + P * t + P], x_rows[:, t, P * k:P * k + P], P)
                if b != 2:
                    ins.then_inc(turned.sem, 1)
            for b in range(4):
                if b >= 2:
                    need(pe, rows_out, 5 + b - 1)
                for k in (2 * b, 2 * b + 1):
                    for t in range(2):
                        ins = turn(ps[:, 6 + b % 2, 256 * (k % 2) + P * t:256 * (k % 2) + P * t + P], ctx_rows[:, t, P * k:P * k + P], P)
                ins.then_inc(turned.sem, 1)
            need(pe, rows_out, 1)
            for l in range(2):
                ins = turn(ps[:, 0, 72 * l:72 * l + 72], bada_rows[:, l, :], 72)
            ins.then_inc(turned.sem, 1)
            need(pe, rows_out, 12)
            norm("mix1", T1)
            linear(st_in1, T1, norm_of["mix1"]["lo"])

            done(pe, "low_split")
            for k in range(KD):
                for w, m in ((glr_hi, u_hi), (glr_hi, u_lo), (glr_lo, u_hi)):
                    ins = mm(ps[:, 4, 0:T1], w[:, k, :], m[:, k, 0:T1], start=(k == 0 and w is glr_hi and m is u_hi),
                             stop=(k == KD - 1 and w is glr_lo))
            ins.then_inc(ev["low_sum"], 1)
            done(pe, "low_out")
            for t in range(2):
                ins = mm(ps[:, 4 + t, 0:T1], wgu[:, P * t:P * t + P], glr[0:16, :], start=True, stop=True)
            ins.then_inc(ev["z_sum"], 1)
            done(pe, "windows")
            done(pe, "b_sum")
            for g, w in enumerate((win_b, win_a, win_b, win_a)):
                mm(ps[:, 4 + g, 0:T1], poolw[:, g, :], w[:, g, PAD:PAD + T1], start=True, stop=True).then_inc(ev["pooled_sum"], 1)
            done(pe, "keys")
            pe.wait_ge(acc_free.sem, 8)
            for n, (c0, L) in enumerate(CHUNKS):
                if n >= 2:
                    done(pe, "chunk_rows", n - 1)
                for h in range(4):
                    turn(ps[0:L, 2 * (n % 2), P * h:P * h + P], proj1[:, 8 + h, c0:c0 + L], P)
                for t in range(2):
                    ins = turn(ps[0:L, 1 + 2 * (n % 2), P * t:P * t + P], kend[:, t, c0:c0 + L], P)
                ins.then_inc(ev["chunk_turned"], 1)
            for n, (c0, L) in enumerate(CHUNKS):
                if n == 0:
                    done(pe, "pooled_out", 4)
                if n >= 1:
                    done(pe, "scores_out", n)
                if n >= 2:
                    done(pe, "state", n - 1)
                done(pe, "chunk_rows", n + 1)
                for h in range(4):
                    ins = mm(ps[0:L, 6, HD * h:HD * h + L], kt[:, h // 2, c0:c0 + L], qz[:, h, c0:c0 + L],
                             start=True, stop=True)
                ins.then_inc(ev["scores"], 1)
                if n < len(CHUNKS) - 1:
                    for h in range(4):
                        ins = mm(ps[:, 4 + n % 2, P * h:P * h + P], k_tok[0:L, n, P * (h // 2):P * (h // 2) + P],
                                 v_tok[0:L, n, P * h:P * h + P], start=True, stop=True)
                    ins.then_inc(ev["chunk_state"], 1)
                done(pe, "causal", n + 1)
                if n:
                    done(pe, "state", n)
                if n:
                    done(pe, "o_out", n)
                for h in range(4):
                    ins = mm(ps[:, 7, HD * h:HD * h + L], v_tok[0:L, n, P * h:P * h + P], sT[0:L, n % 2, h, 0:L],
                             start=True, stop=(n == 0))
                    if n:
                        ins = mm(ps[:, 7, HD * h:HD * h + L], S[:, h, :], qz[:, h, c0:c0 + L], start=False, stop=True)
                ins.then_inc(ev["o_sum"], 1)
            done(pe, "o_sq")
            for h in range(4):
                ins = mm(ps[:, h, 0:T1], ones_d, proj1[:, h, :], start=True, stop=True)
            ins.then_inc(ev["o_ms"], 1)
            done(pe, "o_root")
            linear(st_out1, T1, y_ready[0])

            pe.wait_ge(acc_free.sem, 12)
            norm("ffn1", T1)
            done(pe, "r_split")
            nl = norm_of["ffn1"]["lo"]
            pe.wait_ge(nl.sem, nl.at(8))
            for t, c0 in enumerate((0, P, T1 - P)):
                for k in range(KD):
                    for w, m in ((wr_hi, u_hi), (wr_lo, u_hi), (wr_hi, u_lo)):
                        ins = mm(ps[:, 6, 20 * t:20 * t + 20], m[:, k, c0:c0 + P], w[:, k, :],
                                 start=(k == 0 and w is wr_hi and m is u_hi), stop=(k == KD - 1 and m is u_lo))
            ins.then_inc(ev["logits"], 1)
            done(pe, "shares")
            for t in range(3):
                ins = turn(ps[0:16, 7, P * t:P * t + P], r16[:, t, :], P)
            ins.then_inc(ev["shares_turned"], 1)
            done(pe, "shares_out")
            for e in range(N_EXPERTS):
                if e >= 4:
                    done(pe, "share_out", e - 3)
                mm(ps[:, 4 + e % 4, 0:T1], ident[0:16, e:e + 1].to_broadcast([16, P]), combT[:, :], start=True,
                   stop=True).then_inc(ev["share_sum"], 1)
            done(pe, "share_out", 16)
            ffn_up(st_moe_a, T1, MOE_F, nl, None)
            ffn_down(st_moe_b, moe_sig, T1, 16, hm_hi, hm_lo, MOE_F, "moe_b")
            norm("end1", SEQ)
            for l in range(2):
                L, A = layers[l], attn[l]
                last = l == 1
                TQ = SEQ if last else T2
                norm(f"l{l}a", T2)
                ffn_up(L["f1a"], T2, FFN_F, norm_of[f"l{l}a"]["lo"], None if last else "f1a")
                ffn_down(L["f1b"], L["sig"][0], T2, 11, hf_hi, hf_lo, FFN_F, None if last else "f1b")
                norm(f"l{l}b", T2)
                linear(L["q"], TQ, norm_of[f"l{l}b"]["lo"])
                linear(L["kv"], T2, norm_of[f"l{l}b"]["lo"])
                pe.wait_ge(ld_att, (l + 1) * 16 * (2 + GRID_H * C_HEADS))
                for i, t in enumerate(NORM_TILES):
                    Tn = T2 if t == KB else TQ
                    need(pe, A["pre_act"], 2 * i + 1)
                    mm(ps[:, 4, 0:Tn], bd, tmp_b[:, 0, 0:Tn], start=True, stop=True).then_inc(A["pre_pe"].sem, 1)
                for i, t in enumerate(V_TILES):
                    if i >= 2:
                        need(pe, A["pre_act"], 6 + i - 1)
                    for j in range(4):
                        ins = turn(ps[:, 6 + i % 2, P * j:P * j + P], proj2[:, t, P * j:P * j + P], P)
                    ins.then_inc(A["pre_pe"].sem, 1)
                need(pe, acc_free, end_of(L["kv"]))
                for i in range(6):
                    if i == 5:
                        need(pe, A["bias_out"], 1)
                    mm(ps[:, BIAS_BANKS[i], :], mirror, bias_rev[:, i // 3, 512 * (i % 3):512 * (i % 3) + 512],
                       start=True, stop=True).then_inc(A["bias"].sem, 1)
                need(pe, A["pre_act"], 6 + 5)
                need(pe, A["pre_dve"], 6)
                for i, t in enumerate(ROPE_TILES):
                    if i >= 2:
                        need(pe, A["pre_dve"], 6 + 3 * (i - 1))
                    mm(ps[:, 6 + i % 2, 0:SEQ], rot, proj2[:, t, 0:SEQ], start=True, stop=True).then_inc(A["pre_pe"].sem, 1)
                need(pe, A["pre_act"], 6 + 5 + 1)

                def scores(i):
                    n, q0, k0, nk = A["items"][i]
                    off = HD * (n % 2)
                    if i >= 2:
                        need(pe, A["exped"], i - 1)
                    for q in range(2):
                        c = q0 + P * q
                        ins = mm(ps[:, 2 * (i % 2) + q, 0:nk], proj2[off:off + HD, n // 2, c:c + P],
                                 key_tile(n)[:, k0:k0 + nk], start=True, stop=True)
                    ins.then_inc(A["scores"].sem, 1)

                def turns(i):
                    n, q0, k0, nk = A["items"][i]
                    x = i % 2
                    need(pe, A["probs"], i + 1)
                    if i >= 1:
                        need(pe, A["pt"], i)
                    for j in range(nk // P):
                        for q in range(2):
                            ins = turn(ps[:, 4 + j // 2, 256 * (j % 2) + P * q:256 * (j % 2) + P * q + P],
                                       s[:, x, q, P * j:P * j + P], P)
                    ins.then_inc(A["turned"].sem, 1)

                def values(i):
                    n, q0, k0, nk = A["items"][i]
                    x, off = i % 2, HD * (n % 2)
                    need(pe, A["pt"], i + 1)
                    if i >= 2:
                        need(pe, A["ylo"], i - 1)
                    for j in range(nk // P):
                        ins = mm(ps[off:off + HD, 6 + x, 0:256], value_cols(n, k0 // P + j), pT[:, x, j, :],
                                 start=(j == 0), stop=(j == nk // P - 1))
                    ins.then_inc(A["o"].sem, 1)

                N = len(A["items"])
                scores(0)
                for i in range(N + 1):
                    if i + 1 < N:
                        scores(i + 1)
                    if i < N:
                        turns(i)
                    if i >= 1:
                        values(i - 1)
                need(pe, A["ylo"], N)
                linear(L["out"], TQ, norm_of[f"l{l}b"]["lo"])
                norm(f"l{l}c", TQ)
                ffn_up(L["f2a"], TQ, FFN_F, norm_of[f"l{l}c"]["lo"], None if last else "f2a")
                ffn_down(L["f2b"], L["sig"][1], TQ, 11, hf_hi, hf_lo, FFN_F, None if last else "f2b")
            norm("end2", SEQ)
            src = h2
            w = norm_of["end2"]["w"]
            pe.wait_ge(w.sem, w.at(8))
            for t in range(4):
                for k in range(4):
                    kk = 4 * (t % 2) + k
                    c = P * (t // 2)
                    ins = turn(ps[:, 2 + t, P * k:P * k + P], src[:, kk, c:c + P], P)
                ins.then_inc(turned.sem, 1)


_INS = ["x", "meta_tokens", "norm_mix_w", "w_in", "w_gate_up", "b_gate", "gla_norm_w", "pool_w", "pool_scale", "w_out",
        "norm_ffn_w", "w_router_group", "b_router_group", "w_router_expert", "b_router_expert", "w_expert_gate",
        "w_expert_up", "w_expert_down", "final_norm_w", "c_2", "ctx_2", "c_ctx_2", "w_ada_2", "b_ada_2", "norm_ffn1_2",
        "w_ffn1_gate_2", "w_ffn1_up_2", "w_ffn1_down_2", "norm_mix_2", "w_in_2", "q_norm_glob_2", "k_norm_glob_2",
        "sink_win_2", "rpb_nbr_2", "w_out_2", "norm_ffn2_2", "w_ffn2_gate_2", "w_ffn2_up_2", "w_ffn2_down_2",
        "norm_final_2"]


def kernel(**inputs):
    import concourse.bacc as bacc
    from concourse.bass_utils import run_bass_kernel_spmd

    nc = bacc.Bacc("TRN2", target_bir_lowering=False, num_devices=1, dynamic_dma_scratch_size=1024)
    arrays, a = {}, {}

    def given(name, x):
        x = np.ascontiguousarray(x)
        arrays[f"in_{name}"] = x
        a[name] = nc.dram_tensor(f"in_{name}", x.shape, F32, kind="ExternalInput").ap()

    for name in _INS:
        given(name, inputs[name])
    for name, table in zip(("base", "att", "cnt"), shape_constants()):
        given(name, table)
    out = nc.dram_tensor("out", (1, SEQ, D), F32, kind="ExternalOutput").ap()

    def by_rows(x):
        flat = x
        while len(flat.shape) > 1:
            dims = "abcd"[:len(flat.shape)]
            flat = flat.rearrange(" ".join(dims) + " -> (" + " ".join(dims) + ")")
        return flat.rearrange("(r c) -> r c", c=P)

    a["vec_src"] = [(n, by_rows(a[k])) for n, k in (
        ("c", "c_2"), ("c_ctx", "c_ctx_2"), ("norm_mix", "norm_mix_w"), ("norm_ffn", "norm_ffn_w"), ("final", "final_norm_w"),
        ("pool_scale", "pool_scale"), ("gla_norm", "gla_norm_w"), ("b_gate", "b_gate"), ("ffn1", "norm_ffn1_2"),
        ("mix", "norm_mix_2"), ("ffn2", "norm_ffn2_2"), ("final2", "norm_final_2"))]
    a["vec_src"] += [("q_norm", a["q_norm_glob_2"]), ("k_norm", a["k_norm_glob_2"])]
    program(nc, a, out)
    got = run_bass_kernel_spmd(nc, [arrays], core_ids=[0])
    return got.results[0]["out"]
```

```python
from contextlib import ExitStack

import numpy as np
import concourse.bass as bass
from concourse import mybir

ALU = mybir.AluOpType
ACT = mybir.ActivationFunctionType
F32 = mybir.dt.float32
F32R = mybir.dt.float32r
AX_X = mybir.AxisListType.X

P = 128
D = 1024
KD = D // P
N_META, SEQ, CTX = 16, 256, 256
T1 = N_META + SEQ
T2 = SEQ + CTX
EPS = 1e-6
CHUNKS = [(0, N_META)] + [(N_META + 64 * n, 64) for n in range(SEQ // 64)]
WINDOWS = (2, 4, 8, 16)
PAD = 16
N_GROUPS, PER_GROUP = 4, 4
N_EXPERTS = N_GROUPS * PER_GROUP
HID = D // 4
MOE_F = N_EXPERTS * HID // P
FFN_F = 2816 // P
HD = 64
GRID_W, NA_KH, NA_KW = 64, 8, 16
GRID_H = SEQ // GRID_W
RPB_W = 2 * NA_KW - 1
RPB_H = 2 * NA_KH - 1
NEG = -1e30
A_HEADS, B_HEADS, C_HEADS = 6, 4, 6
HEADS = A_HEADS + B_HEADS + C_HEADS
KA, VA, KB, VB, KC, VC = 8, 9, 10, 11, 12, 15
V_TILES = [VA, VB, VC, VC + 1, VC + 2]
PROJ2 = 18
ROPE_TILES = [0, 1, 2, KA, 3, 4, KB]
NORM_TILES = [3, 4, KB]
UNIT = 16 * P
ADA_COLS = 512
ADA_CHUNKS = 9 * D // ADA_COLS

VEC = {}
for _name, _rows in (("c", 8), ("c_ctx", 8), ("norm_mix", 8), ("norm_ffn", 8), ("final", 8), ("pool_scale", 4),
                     ("gla_norm", 1), ("b_gate", 2), ("ffn1", 16), ("mix", 16), ("ffn2", 16), ("final2", 8),
                     ("q_norm", 2), ("k_norm", 2)):
    VEC[_name] = (sum(n for _, n in VEC.values()), _rows)
VEC_ROWS = sum(n for _, n in VEC.values())


def shape_constants():
    p = np.arange(P)
    base = np.zeros((P, 264), np.float32)
    base[:, 0:128] = np.eye(P)
    base[:, 128:256] = 1.0 / D
    base[:, 256] = 1.0
    base[:, 257] = EPS
    base[:, 258:262] = [4, 3, 2, 1]
    block = (p[:, None] // HD == p[None, :] // HD) / HD
    half = HD // 2
    rot = np.zeros((P, P))
    for m in range(P):
        if m % HD < half:
            rot[m + half, m] = -1.0
        else:
            rot[m - half, m] = 1.0
    t = np.arange(SEQ)
    n_freq = HD // 4
    inv = np.float32(10000.0) ** (-np.arange(n_freq, dtype=np.float32) / n_freq)
    ang = np.concatenate([(t // GRID_W).astype(np.float32)[:, None] * inv,
                          (t % GRID_W).astype(np.float32)[:, None] * inv], axis=-1)
    cos, sin = np.cos(ang).T[p % half], np.sin(ang).T[p % half]
    q = np.arange(2)[None, :, None] * P + p[:, None, None]
    win = np.zeros((P, 2, T2))
    win[:, :, :SEQ] = np.where(np.abs(np.arange(SEQ)[None, None, :] - q) <= 128, 0.0, NEG)
    col = np.clip(p % GRID_W - NA_KW // 2, 0, GRID_W - NA_KW)[:, None]
    key = (t % GRID_W)[None, :]
    nbr = np.where((key >= col) & (key < col + NA_KW), 0.0, NEG)
    mirror = (p[:, None] == (p[None, :] // GRID_W) * GRID_W + GRID_W - 1 - p[None, :] % GRID_W)
    att = np.concatenate([block, rot, cos, sin, win.reshape(P, -1), nbr, mirror], axis=1).astype(np.float32)
    tok = np.arange(T1)
    cnt = np.stack([1.0 / np.minimum(tok + 1, w) for w in WINDOWS]).astype(np.float32)
    return base, att, np.broadcast_to(cnt.reshape(1, -1), (P, 4 * T1)).copy()


class Signal:

    def __init__(self, sem, base):
        self.sem, self.base = sem, base

    def at(self, n):
        return self.base + n


def repeat(eng, n, body):
    if n <= 3:
        for i in range(n):
            body(i)
        return
    body(0)
    with eng.Fori(1, n - 1) as i:
        body(i)
    body(n - 1)


def program(nc, a, out):
    with ExitStack() as ctx:
        counted = {}

        def sem(name):
            return ctx.enter_context(nc.semaphore(name))

        def signal(role, total):
            if role not in counted:
                counted[role] = [sem(role), 0]
            s, base = counted[role]
            counted[role][1] += total
            return Signal(s, base)

        def need(eng, sig, n=None):
            v = sig.at(n)
            if isinstance(v, int) and v <= 0:
                return
            eng.wait_ge(sig.sem, v)

        def sb(name, shape, dt=F32):
            return ctx.enter_context(nc.sbuf_tensor(name, shape, dt))

        start = (nc.sbuf_base + 31) // 32 * 32
        region_bytes = 4 * 2 * FFN_F * T2
        nc.alloc_sbuf_tensor("region", [P, region_bytes // 4 + 8], F32)
        raw = sb("raw", [P, 2, UNIT])
        w_hi = sb("w_hi", [P, 2, UNIT], F32R)
        w_lo = sb("w_lo", [P, 2, UNIT], F32R)
        u_hi = sb("u_hi", [P, KD, T2], F32R)
        u_lo = sb("u_lo", [P, KD, T2], F32R)
        h1 = sb("h1", [P, KD, T1])
        h2 = sb("h2", [P, KD, T2])
        ada_w = sb("ada_w", [P, 2, 2, ADA_COLS])
        ada_acc = sb("ada_acc", [P, 2, ADA_COLS])
        rstd = sb("rstd", [P, T2])
        tmp_a = sb("tmp_a", [P, 2, T2])
        tmp_b = sb("tmp_b", [P, 2, T2])
        base = sb("base", [P, 264])
        vec = sb("vec", [P, VEC_ROWS])
        b_ada = sb("b_ada", [P, 144, 2])
        mod = sb("mod", [P, 144, 2])
        sc_c = sb("sc_c", [P, KD, 2])
        coef = sb("coef", [P, KD, 2])
        gate = sb("gate", [P, KD, 2])
        root_one = sb("root_one", [P, 1])
        ident, ones_d = base[:, 0:128], base[:, 128:256]
        one, eps, rank = base[:, 256:257], base[:, 257:258], base[:, 258:262]
        ps = ctx.enter_context(nc.psum_tensor("ps", [P, 8, 512], F32))

        R4_at = {}

        def carve(names):
            at, got = start, {}
            R4_at.clear()
            for name, shape, dt in names:
                size = 4 * int(np.prod(shape[1:]))
                got[name] = nc.alloc_sbuf_tensor_at(name, shape, dt, offset=at)
                R4_at[name] = at
                at += (size + 31) // 32 * 32
            assert at - start <= region_bytes, (at - start, names)
            return got

        R0 = carve([("x_rows", [P, 2, D], F32), ("meta_rows", [N_META, D], F32), ("ctx_rows", [P, 2, D], F32),
                    ("vec_rows", [VEC_ROWS, P], F32), ("bada_rows", [72, 2, P], F32)])
        R1 = carve([("proj1", [P, 16, T1], F32), ("glr_raw", [P, KD, P], F32), ("glr_hi", [P, KD, P], F32R),
                    ("glr_lo", [P, KD, P], F32R), ("glr", [P, T1], F32), ("wgu", [16, 256], F32),
                    ("win_a", [P, 4, PAD + T1], F32), ("win_b", [P, 4, PAD + T1], F32), ("cnt", [P, 4, T1], F32),
                    ("poolw", [P, 4, P], F32), ("lga", [P, 2, T1], F32), ("lgb", [P, 2, T1], F32),
                    ("qz", [P, 4, T1], F32), ("kt", [P, 2, T1], F32), ("kend", [P, 2, T1], F32),
                    ("v_tok", [64, 5, 512], F32), ("k_tok", [64, 5, 256], F32), ("sT", [64, 2, 4, 64], F32),
                    ("S", [P, 4, P], F32)])
        RG = carve([("g_pad", [P, 16, T1], F32), ("oT", [P, 4, T1], F32)])
        R2 = carve([("hm_hi", [P, MOE_F, T1], F32R), ("hm_lo", [P, MOE_F, T1], F32R), ("comb", [P, N_EXPERTS, T1], F32)])
        RR = carve([("wr", [P, KD, 20], F32), ("wr_hi", [P, KD, 20], F32R), ("wr_lo", [P, KD, 20], F32R),
                    ("rb", [P, 20], F32), ("lg", [P, 3, 20], F32), ("r4a", [P, 3, 4], F32), ("r4b", [P, 3, 4], F32),
                    ("r4c", [P, 3, 4], F32), ("oh_g", [P, 3, 4], F32), ("r1a", [P, 3], F32), ("r1b", [P, 3], F32),
                    ("r1c", [P, 3], F32), ("pg", [P, 3], F32), ("r16", [P, 3, 16], F32), ("oh1", [P, 3, 4], F32),
                    ("prob", [P, 3, 4], F32), ("combT", [16, T1], F32), ("lgT", [20, T1], F32),
                    ("comb_hi", [16, T1], F32R), ("comb_lo", [16, T1], F32R), ("pick", [16, 16], F32R)])
        R3 = carve([("hf_hi", [P, FFN_F, T2], F32R), ("hf_lo", [P, FFN_F, T2], F32R)])
        R4 = carve([("proj2", [P, PROJ2, T2], F32), ("k_sw", [P, 2, T2], F32), ("vt", [P, 5, 4, P], F32),
                    ("s", [P, 2, 2, T2], F32), ("pT", [P, 2, 4, 256], F32), ("bias_c", [P, 2, C_HEADS, SEQ], F32),
                    ("att", [P, 2176], F32), ("sink", [P, A_HEADS], F32), ("st", [P, 2, 8], F32)])
        bias_rev = nc.alloc_sbuf_tensor_at("bias_rev", [P, 2, C_HEADS * SEQ], F32, offset=R4_at["s"])
        RO = carve([("o_rows", [P, 2, D], F32)])
        x_rows, meta_rows, ctx_rows, vec_rows, bada_rows = R0.values()
        (proj1, glr_raw, glr_hi, glr_lo, glr, wgu, win_a, win_b, cnt, poolw, lga, lgb, qz, kt, kend, v_tok, k_tok,
         sT, S) = R1.values()
        oT = RG["oT"]
        hm_hi, hm_lo, comb = R2.values()
        wr, wr_hi, wr_lo, rb, lg, r4a, r4b, r4c, oh_g, r1a, r1b, r1c, pg, r16, oh1, prob, combT, lgT, comb_hi, comb_lo, pick = RR.values()
        hf_hi, hf_lo = R3.values()
        proj2, k_sw, vt, s, pT, bias_c, att, sink, st = R4.values()
        o_rows = RO["o_rows"]
        bd, rot = att[:, 0:128], att[:, 128:256]
        cos, sin = att[:, 256:512], att[:, 512:768]
        win_mask = att[:, 768:1792].rearrange("p (q k) -> p q k", q=2)
        nbr_mask, mirror = att[:, 1792:2048], att[:, 2048:2176]

        stream = []

        def streamed(name, units, groups, elems):
            u0 = sum(x["units"] for x in stream)
            g0 = sum(x["groups"] for x in stream)
            d = dict(name=name, units=units, groups=groups, elems=elems, u0=u0, g0=g0)
            stream.append(d)
            return d

        st_in1 = streamed("in1", 8, 8, UNIT)
        st_out1 = streamed("out1", 4, 4, UNIT)
        st_moe_a = streamed("moe_a", MOE_F, MOE_F, UNIT)
        st_moe_b = streamed("moe_b", 16, 8, UNIT)
        layers = []
        for l in range(2):
            layers.append(dict(
                f1a=streamed("f1a", FFN_F, FFN_F, UNIT), f1b=streamed("f1b", 16, 8, 11 * P),
                q=streamed("q", 4, 4, UNIT), kv=streamed("kv", 5, 5, UNIT), out=streamed("out", 4, 4, UNIT),
                f2a=streamed("f2a", FFN_F, FFN_F, UNIT), f2b=streamed("f2b", 16, 8, 11 * P)))
        elems_of = [x["elems"] for x in stream for _ in range(x["units"])]
        N_UNITS = len(elems_of)

        def end_of(stg):
            return stg["g0"] + stg["groups"]

        raw_full = [sem("raw_full_0"), sem("raw_full_1")]
        hi_done = signal("hi_done", 0)
        lo_done = signal("lo_done", 0)
        unit_done = signal("unit_done", 0)
        acc_free = signal("acc_free", 0)
        ada_full = [sem("ada_full_0"), sem("ada_full_1")]
        ada_mac = signal("ada_mac", 0)
        ada_sum = signal("ada_sum", 0)
        mod_done = signal("mod_done", 0)
        dve_chain = signal("dve_chain", 0)
        act_chain = signal("act_chain", 0)
        pool_chain = signal("pool_chain", 0)
        pe_chain = signal("pe_chain", 0)

        ld_rows, ld_x, ld_ctx = sem("ld_rows"), sem("ld_x"), sem("ld_ctx")
        ld_small = sem("ld_small")
        ld_router, ld_att, ld_bias, st_out = sem("ld_router"), sem("ld_att"), sem("ld_bias"), sem("st_out")
        N_ROWS = 1 + len(VEC) + 2 + 2

        norms = []
        for name in ("mix1", "ffn1", "end1", "l0a", "l0b", "l0c", "l1a", "l1b", "l1c", "end2"):
            norms.append(dict(name=name, sq=signal("norm_sq", 8), ms=signal("norm_ms", 8), root=signal("norm_root", 1),
                              rstd=signal("norm_rstd", 1), t=signal("norm_t", 8), w=signal("norm_w", 8),
                              hi=signal("norm_hi", 0 if "end" in name else 8),
                              lo=signal("norm_lo", 0 if "end" in name else 8)))
        norm_of = {n["name"]: n for n in norms}

        def ffn_signals(n, weighted=False):
            return dict(silu=signal("silu", n), comb=signal("weighted", n if weighted else 0), hi=signal("hidden_hi", n),
                        lo=signal("hidden_lo", n))

        moe_sig = ffn_signals(MOE_F, True)
        ffn_sig = [[ffn_signals(FFN_F), ffn_signals(FFN_F)] for _ in range(2)]
        for l in range(2):
            layers[l]["sig"] = ffn_sig[l]

        turned = signal("turned", 12)
        rows_out = signal("rows_out", 12)
        y_ready = [signal("y_ready", 8)]
        ev = {k: sem("ev_" + k) for k in (
            "low_zero", "low_split", "low_sum", "low_out", "win_zero", "windows", "z_sum", "z_ln", "b_sum", "exps",
            "keys", "pooled_sum", "pooled_out", "chunk_turned", "chunk_rows", "scores", "scores_out", "causal",
            "o_sum", "o_out", "chunk_state", "state", "silu_r", "o_sq", "o_ms", "o_root", "r_split", "gla_out", "gla_hi", "gated", "logits", "logits_out", "logits_turned", "g_shift", "g_exp",
            "e_shift", "e_exp", "shares", "shares_turned", "shares_out", "share_sum", "share_out", "share_out_odd")}

        def row(h, m, c0, c1):
            return h[:, m, c0:c1] if isinstance(m, int) else h[:, bass.ds(m, 1), c0:c1].rearrange("p o t -> p (o t)")

        def items(l):
            it = [(n, 0, 0, T2) for n in range(HEADS)]
            if l == 0:
                it += [(n, SEQ, SEQ, CTX) for n in range(HEADS)]
            return it

        attn = []
        for l in range(2):
            n = len(items(l))
            attn.append(dict(
                items=items(l), pre_sq=signal("at_pre_sq", 3), pre_pe=signal("at_pre_pe", 15), pre_act=signal("at_pre_act", 8),
                pre_inv=signal("at_pre_inv", 3), normed=signal("at_normed", 3), rot=signal("at_rotated", 7),
                roped=signal("at_roped", 7), k_sw=signal("at_k_sw", 1),
                bias=signal("at_bias", 6), bias_out=signal("at_bias_out", 6), scores=signal("at_scores", n), logits=signal("at_logits", n),
                exped=signal("at_exped", n), probs=signal("at_probs", n), turned=signal("at_turned", n),
                pt=signal("at_pt", n), o=signal("at_o", n), yhi=signal("at_yhi", n), ylo=signal("at_ylo", n)))

        BIAS_BANKS = [0, 1, 2, 3, 4, 0]

        PRE = {1: [("norm", 3), ("norm", 4), ("value", VA)], 2: [("norm", KB), ("value", VB), ("rope", 0)],
               3: [("rope", 1), ("rope", 2), ("rope", KA)], 4: [("rope", 3), ("rope", 4), ("rope", KB)],
               5: [("value", VC), ("value", VC + 1), ("value", VC + 2)]}
        PRE_ORDER = [x for i in sorted(PRE) for x in PRE[i]]

        def pre_bank(x):
            return 5 + PRE_ORDER.index(x) % 3

        def pre_count(kinds, end):
            return sum(k in kinds for k, _ in PRE_ORDER[:end])

        def taken_with(tile):
            return 0 if tile < KA else (tile - KA) // 2 + 1

        def kind(n):
            return "A" if n < A_HEADS else "B" if n < A_HEADS + B_HEADS else "C"

        def key_tile(n):
            off = HD * (n % 2)
            if kind(n) == "C":
                m = n - A_HEADS - B_HEADS
                return proj2[off:off + HD, KC + m // 2, :]
            kv = n // 3 if kind(n) == "A" else (n - A_HEADS) // 2
            which = 0 if kind(n) == "A" else 1
            if HD * kv == off:
                return proj2[off:off + HD, KA if which == 0 else KB, :]
            return k_sw[off:off + HD, which, :]

        def value_cols(n, j):
            if kind(n) == "A":
                t, kv = 0, n // 3
            elif kind(n) == "B":
                t, kv = 1, (n - A_HEADS) // 2
            else:
                m = n - A_HEADS - B_HEADS
                t, kv = 2 + m // 2, m % 2
            return vt[:, t, j, HD * kv:HD * kv + HD]

        ADA = {"moe_b": (1, 1), "f1a": (5, 1), "f1b": (10, 1), "f2a": (17, 2), "f2b": (27, 1), "l1_f1a": (31, 1)}
        ADA_LINEAR = {"in1": (0, 1, 4), "q": (14, 2, 2), "out": (16, 1, 2), None: (0, 0, 1)}

        def ada_of_unit(ada, i):
            first, count, share = ADA_LINEAR[ada]
            per = 4 // share
            c = i // share
            work = [(first + c, per * (i % share) + q) for q in range(per)] if c < count else []
            return work, first + c - 1 if i % share == 0 and 1 <= c <= count else None

        def ada_plan(chunks):
            if chunks == 0:
                return [([], None)] * 4
            if chunks == 1:
                return [([(0, j)], -1 if j == 0 else None) for j in range(4)]
            return [([(j // 2, 2 * (j % 2)), (j // 2, 2 * (j % 2) + 1)], {0: -1, 2: 0}.get(j)) for j in range(4)]

        block = ctx.enter_context(nc.Block())

        @block.sync
        def _(sp):
            def rows(dst, src, s):
                sp.dma_start(dst, src).then_inc(s, 16)

            rows(base[:, :], a["base"], ld_rows)
            for name, src in a["vec_src"]:
                r0, n = VEC[name]
                if name in ("q_norm", "k_norm"):
                    rows(vec_rows[r0:r0 + n, 0:HD], src, ld_rows)
                    rows(vec_rows[r0:r0 + n, HD:2 * HD], src, ld_rows)
                else:
                    rows(vec_rows[r0:r0 + n, :], src, ld_rows)
            for l in range(2):
                rows(bada_rows[:, l, :], a["b_ada_2"][l].rearrange("(r c) -> r c", c=P), ld_rows)
            rows(x_rows[:, :, :], a["x"][0].rearrange("(t p) d -> p t d", p=P), ld_x)
            rows(meta_rows[:, :], a["meta_tokens"], ld_x)
            rows(ctx_rows[:, :, :], a["ctx_2"][0].rearrange("(t p) d -> p t d", p=P), ld_x)

            def unit(u, slot, parts):
                need(sp, hi_done, u - 1)
                need(sp, lo_done, u - 1)
                for dst, src in parts(raw[:, slot, :]):
                    sp.dma_start(dst, src).then_inc(raw_full[slot], 16)

            def linear(stg, w, col0=0, units=None):
                wv = w.rearrange("(k p) n -> p k n", p=P)
                for i in units or range(stg["units"]):
                    def parts(r, i=i):
                        v = r.rearrange("p (k n) -> p k n", k=KD)
                        c = col0 + 2 * P * i
                        return [(v[:, 0:4, :], wv[:, 0:4, c:c + 2 * P]), (v[:, 4:8, :], wv[:, 4:8, c:c + 2 * P])]
                    unit(stg["u0"] + i, (stg["u0"] + i) % 2, parts)

            def gate_up(stg, src_of, n_units):
                def step(i, j):
                    u = stg["u0"] + 4 * i + j
                    def parts(r):
                        v = r.rearrange("p (m k n) -> p m k n", m=2, k=KD)
                        g, up = src_of(i, j)
                        return [(v[:, 0], g), (v[:, 1], up)]
                    unit(u, (stg["u0"] + j) % 2, parts)
                def body(i):
                    for j in range(4):
                        step(i, j)
                repeat(sp, n_units // 4, body)
                for j in range(n_units % 4):
                    step(n_units // 4, j)

            def down(stg, w, kt2):
                wv = w.rearrange("(k p) n -> p k n", p=P)
                half = (kt2 + 1) // 2
                def body(i):
                    for j in range(4):
                        u = stg["u0"] + 4 * i + j
                        def parts(r, j=j):
                            v = r.rearrange("p (k n) -> p k n", n=P)
                            k0 = kt2 * (j % 2)
                            cols = bass.ds(i * (2 * P) + P * (j // 2), P)
                            return [(v[:, 0:half, :], wv[:, k0:k0 + half, cols]),
                                    (v[:, half:kt2, :], wv[:, k0 + half:k0 + kt2, cols])]
                        unit(u, (stg["u0"] + j) % 2, parts)
                repeat(sp, 4, body)

            linear(st_in1, a["w_in"][0])
            sp.wait_ge(rows_out.sem, rows_out.at(12))
            sp.wait_ge(ev["low_zero"], 1)
            sp.dma_start(glr_raw[:, :, 0:16], a["w_in"][0].rearrange("(k p) n -> p k n", p=P)[:, :, 2048:2064]).then_inc(ld_small, 16)
            sp.dma_start(wgu[:, :], a["w_gate_up"][0]).then_inc(ld_small, 16)
            sp.dma_start(cnt[:, :, :], a["cnt"].rearrange("p (g t) -> p g t", g=4)).then_inc(ld_small, 16)
            sp.dma_start(poolw[:, :, :], a["pool_w"][0].rearrange("g c d -> c g d")).then_inc(ld_small, 16)
            linear(st_out1, a["w_out"][0])
            sp.wait_ge(y_ready[0].sem, y_ready[0].at(8))
            wrv = wr[:, :, :]
            sp.dma_start(wrv[:, :, 0:4], a["w_router_group"][0].rearrange("(k p) n -> p k n", p=P)).then_inc(ld_router, 16)
            sp.dma_start(wrv[:, :, 4:20], a["w_router_expert"][0].rearrange("(k p) n -> p k n", p=P)).then_inc(ld_router, 16)
            sp.dma_start(rb[:, 0:4], a["b_router_group"][0:1, :].to_broadcast([P, 4])).then_inc(ld_router, 16)
            sp.dma_start(rb[:, 4:20], a["b_router_expert"][0:1, :].to_broadcast([P, 16])).then_inc(ld_router, 16)

            def experts(i, j):
                got = []
                for w in (a["w_expert_gate"], a["w_expert_up"]):
                    wv = w[0].rearrange("e (k p) n -> p e k n", p=P)
                    v = wv[:, bass.ds(2 * i + j // 2, 1), :, P * (j % 2):P * (j % 2) + P]
                    got.append(v.rearrange("p o k n -> p (o k) n"))
                return got
            gate_up(st_moe_a, experts, MOE_F)
            down(st_moe_b, a["w_expert_down"][0].rearrange("e f d -> (e f) d"), 16)
            for l in range(2):
                L = layers[l]

                def ffn(n):
                    def cols(i, j):
                        c = bass.ds(i * (4 * P) + P * j, P)
                        return [a[f"w_ffn{n}_{m}_2"][l].rearrange("(k p) n -> p k n", p=P)[:, :, c] for m in ("gate", "up")]
                    gate_up(L[f"f{n}a"], cols, FFN_F)
                    down(L[f"f{n}b"], a[f"w_ffn{n}_down_2"][l], 11)
                ffn(1)
                linear(L["q"], a["w_in_2"][l], 0)
                sp.wait_ge(acc_free.sem, L["q"]["g0"])
                sp.dma_start(att[:, :], a["att"]).then_inc(ld_att, 16)
                sp.dma_start(sink[:, :], a["sink_win_2"][l:l + 1, :].to_broadcast([P, A_HEADS])).then_inc(ld_att, 16)
                linear(L["kv"], a["w_in_2"][l], D, range(0, 3))
                for r in range(GRID_H):
                    rp = a["rpb_nbr_2"]
                    off = (l * C_HEADS * RPB_H + NA_KH - 1 - r) * RPB_W + NA_KW - 1 - (GRID_W - 1)
                    p0 = GRID_W * (r % 2)
                    for h in range(C_HEADS):
                        src = bass.AP(rp.tensor, off + h * RPB_H * RPB_W, [[1, GRID_W], [RPB_W, GRID_H], [1, GRID_W]])
                        dst = bias_rev[p0:p0 + GRID_W, r // 2, SEQ * h:SEQ * h + SEQ]
                        sp.dma_start(dst.rearrange("p (r c) -> p r c", r=GRID_H), src).then_inc(ld_bias, 16)
                linear(L["kv"], a["w_in_2"][l], D, range(3, 5))
                linear(L["out"], a["w_out_2"][l])
                ffn(2)
            sp.wait_ge(rows_out.sem, rows_out.at(12 + 4))
            sp.dma_start(out[0].rearrange("(t p) d -> p t d", p=P), o_rows[:, :, :]).then_inc(st_out, 16)
            sp.wait_ge(st_out, 16)

        @block.scalar
        def _(act):
            chain = [0]

            def link(ins):
                chain[0] += 1
                ins.then_inc(act_chain.sem, 1)
                act.wait_ge(act_chain.sem, chain[0])

            def split_hi(u, slot, elems):
                if isinstance(u, int) and u >= N_UNITS:
                    return
                act.wait_ge(raw_full[slot], 32 * (u // 2) + 32 if isinstance(u, int) else u * 16 + (32 - 16 * slot))
                need(act, unit_done, u - 1)
                nc.scalar.copy(w_hi[:, slot, 0:elems], raw[:, slot, 0:elems]).then_inc(hi_done.sem, 1)

            def next_hi(stg, i, j, per=4):
                u = stg["u0"] + per * i + j + 2
                slot = (stg["u0"] + j) % 2
                if isinstance(u, int):
                    if u < N_UNITS:
                        split_hi(u, slot, elems_of[u])
                else:
                    split_hi(u, slot, stg["elems"])

            def ada_load(l, j, quarter):
                if isinstance(j, int):
                    l = j // ADA_CHUNKS
                slot = quarter % 2
                q = 4 * j + quarter
                need(act, ada_mac, 4 * (q - 1))
                k = 2 * quarter
                wv = a["w_ada_2"][l].rearrange("(k p) n -> p k n", p=P)
                c = bass.ds((j - ADA_CHUNKS * l) * ADA_COLS, ADA_COLS)
                act.dma_start(ada_w[:, slot, :, :], wv[:, k:k + 2, c]).then_inc(ada_full[slot], 16)

            def square(nm, k, slot, h, T, first=0):
                n = norm_of[nm]
                if not isinstance(k, int) or k >= 2:
                    act.wait_ge(n["ms"].sem, n["ms"].at(k - 1))
                nc.scalar.activation(tmp_b[:, slot, 0:T], row(h, k, first, first + T), ACT.Square).then_inc(n["sq"].sem, 1)

            def linear(stg, squares=None, ada=None, behind=None):
                for i in range(stg["units"]):
                    for c, quarter in ada_of_unit(ada, i)[0]:
                        ada_load(0, c, quarter)
                    if squares and i:
                        act.wait_ge(acc_free.sem, acc_free.at(stg["g0"] + i))
                        for k in (2 * i - 2, 2 * i - 1):
                            square(squares[0], k, k % 2, *squares[1:])
                    u = stg["u0"] + i + 2
                    if u < N_UNITS:
                        split_hi(u, u % 2, elems_of[u])
                    if behind:
                        behind(i)

            def norm(nm, after, h, T, first=0, scale=None, shift=None, dest=None, splits=((0, None),), rows_squared=KD,
                     behind=None):
                n = norm_of[nm]
                need(act, acc_free, after)
                for k in range(rows_squared, KD):
                    square(nm, k, k % 2, h, T, first)
                act.wait_ge(n["ms"].sem, n["ms"].at(KD))
                nc.scalar.activation(rstd[:, 0:T], ps[:, 5, 0:T], ACT.Sqrt, bias=eps).then_inc(n["root"].sem, 1)
                for k in range(KD):
                    act.wait_ge(n["t"].sem, n["t"].at(k + 1))
                    if dest is None and k >= 2:
                        act.wait_ge(n["lo"].sem, n["lo"].at(k - 1))
                    o = tmp_b[:, k % 2, :] if dest is None else dest[:, k, :]
                    for q, (c0, c1) in enumerate(splits):
                        ins = nc.scalar.activation(o[:, c0:c1], tmp_a[:, k % 2, c0:c1], ACT.Identity, scale=scale(k, q),
                                                   bias=shift(k, q) if shift else 0.0)
                    ins.then_inc(n["w"].sem, 1)
                    if behind:
                        act.wait_ge(n["w"].sem, n["w"].at(k + 1))
                        behind(k)

            def ffn_up(stg, sig, T, n_units, hi, l, ada):
                first, per = ADA[ada] if ada else (0, 0)
                plan = ada_plan(per)

                def step(i, j, work):
                    if work:
                        for c, quarter in plan[j][0]:
                            ada_load(l, first + per * i + c, quarter)
                    n = 4 * i + j
                    g = stg["g0"] + j
                    act.wait_ge(unit_done.sem, stg["u0"] + n + 1)
                    need(act, acc_free, stg["g0"] + n - 1)
                    nc.scalar.activation(tmp_a[:, j % 2, 0:T], ps[:, 2 * (g % 2), 0:T], ACT.Silu).then_inc(sig["silu"].sem, 1)
                    next_hi(stg, i, j)
                    act.wait_ge(acc_free.sem, stg["g0"] + n + 1)
                    row = hi[:, n, 0:T] if isinstance(n, int) else hi[:, bass.ds(n, 1), 0:T].rearrange("p o t -> p (o t)")
                    nc.scalar.copy(row, tmp_b[:, j % 2, 0:T]).then_inc(sig["hi"].sem, 1)

                def body(i):
                    for j in range(4):
                        step(i, j, True)
                repeat(act, n_units // 4, body)
                for j in range(n_units % 4):
                    step(n_units // 4, j, False)

            def ffn_down(stg, l, ada, squares):
                first, per = ADA[ada] if ada else (0, 0)
                plan = ada_plan(per)
                nc.scalar.activation(root_one[:, :], one, ACT.Sqrt)

                def body(i):
                    for j in range(4):
                        for c, quarter in plan[j][0]:
                            ada_load(l, first + per * i + c, quarter)
                        k = 2 * i + j // 2 - 1
                        if j % 2 == 0 and not (isinstance(k, int) and k < 0):
                            act.wait_ge(acc_free.sem, acc_free.at(stg["g0"] + k + 1))
                            square(squares[0], k, (j // 2 + 1) % 2, *squares[1:])
                        next_hi(stg, i, j)
                repeat(act, 4, body)

            act.wait_ge(ld_rows, 16 * N_ROWS)
            split_hi(0, 0, UNIT)
            split_hi(1, 1, UNIT)
            act.wait_ge(rows_out.sem, rows_out.at(1))
            nc.scalar.activation(sc_c[:, :, 0], vec[:, 0:8], ACT.Silu)
            nc.scalar.activation(sc_c[:, :, 1], vec[:, 8:16], ACT.Silu).then_inc(act_chain.sem, 1)
            chain[0] += 1

            act.wait_ge(rows_out.sem, rows_out.at(5))
            norm("mix1", 0, h1, T1, scale=lambda k, q: vec[:, VEC["norm_mix"][0] + k:VEC["norm_mix"][0] + k + 1],
                 splits=((0, T1),), rows_squared=0)
            linear(st_in1, ada="in1")

            act.wait_ge(ev["z_sum"], 1)
            bg = VEC["b_gate"][0]
            for t in range(2):
                ins = nc.scalar.activation(lga[:, t, :], ps[:, 4 + t, 0:T1], ACT.Abs, bias=vec[:, bg + t:bg + t + 1])
            link(ins)
            link(nc.scalar.activation(lga[:, :, :], lga[:, :, :], ACT.Exp, scale=-1.0))
            nc.scalar.activation(lga[:, :, :], lga[:, :, :], ACT.Ln, bias=one).then_inc(ev["z_ln"], 1)
            act.wait_ge(ev["b_sum"], 1)
            nc.scalar.activation(lga[:, :, :], lgb[:, :, :], ACT.Exp)
            nc.scalar.activation(kt[:, :, :], lgb[:, :, :], ACT.Exp, scale=-1.0)
            for t in range(2):
                for c0, n in CHUNKS:
                    ins = nc.scalar.activation(kend[:, t, c0:c0 + n], lgb[:, t, c0:c0 + n], ACT.Exp, scale=-1.0,
                                               bias=lgb[:, t, c0 + n - 1:c0 + n])
            ins.then_inc(ev["exps"], 1)
            for n in range(5):
                act.wait_ge(ev["chunk_turned"], n + 1)
                L = CHUNKS[n][1]
                nc.scalar.copy(v_tok[0:L, n, :], ps[0:L, 0 + 2 * (n % 2), :])
                nc.scalar.copy(k_tok[0:L, n, :], ps[0:L, 1 + 2 * (n % 2), 0:256]).then_inc(ev["chunk_rows"], 1)
            nc.scalar.activation(proj1[:, 12:16, :], proj1[:, 12:16, :], ACT.Silu).then_inc(ev["silu_r"], 1)
            act.wait_ge(ev["o_out"], 5)
            nc.scalar.activation(proj1[:, 0:4, :], oT[:, :, :], ACT.Square).then_inc(ev["o_sq"], 1)
            act.wait_ge(ev["o_ms"], 1)
            for h in range(4):
                nc.scalar.activation(proj1[:, 4 + h, :], ps[:, h, 0:T1], ACT.Sqrt, scale=float(D // P),
                                     bias=eps).then_inc(ev["o_root"], 1)
            for h in range(4):
                act.wait_ge(ev["gla_out"], h + 1)
                nc.scalar.copy(u_hi[:, 4 + h, 0:T1], oT[:, h, :]).then_inc(ev["gla_hi"], 1)
            linear(st_out1, ("ffn1", h1, T1))
            norm("ffn1", end_of(st_out1), h1, T1, scale=lambda k, q: vec[:, VEC["norm_ffn"][0] + k:VEC["norm_ffn"][0] + k + 1],
                 splits=((0, T1),), rows_squared=KD - 2)
            act.wait_ge(ev["g_shift"], 1)
            nc.scalar.activation(r4b[:, :, :], r4a[:, :, :], ACT.Exp).then_inc(ev["g_exp"], 1)
            act.wait_ge(ev["e_shift"], 1)
            nc.scalar.activation(prob[:, :, :], r4c[:, :, :], ACT.Exp).then_inc(ev["e_exp"], 1)
            for e in range(0, N_EXPERTS, 2):
                act.wait_ge(ev["share_sum"], e + 1)
                nc.scalar.copy(comb[:, e, :], ps[:, 4 + e % 4, 0:T1]).then_inc(ev["share_out"], 1)
            ffn_up(st_moe_a, moe_sig, T1, MOE_F, hm_hi, 0, None)
            ffn_down(st_moe_b, 0, "moe_b", ("end1", h1, SEQ, N_META))
            fin = VEC["final"][0]
            norm("end1", end_of(st_moe_b), h1, SEQ, first=N_META, scale=lambda k, q: vec[:, fin + k:fin + k + 1], dest=h2, splits=((0, SEQ),), rows_squared=KD - 1,
                 behind=lambda k: square("l0a", k, k % 2, h2, T2))
            both = ((0, SEQ), (SEQ, T2))

            def modulated(nm, after, l, m, T, squared):
                t0 = 72 * l + 8 * m
                norm(nm, end_of(after), h2, T, scale=lambda k, q: coef[:, k, q:q + 1], shift=lambda k, q: mod[:, t0 + k, q:q + 1],
                     splits=both if T == T2 else both[:1], rows_squared=squared)

            for l in range(2):
                L, A = layers[l], attn[l]
                last = l == 1
                TQ = SEQ if last else T2
                modulated(f"l{l}a", layers[0]["f2b"] if last else st_moe_b, l, 0, T2, KD - 1 if last else KD)
                ffn_up(L["f1a"], L["sig"][0], T2, FFN_F, hf_hi, l, "l1_f1a" if last else "f1a")
                ffn_down(L["f1b"], 0, None if last else "f1b", (f"l{l}b", h2, T2))
                modulated(f"l{l}b", L["f1b"], l, 3, T2, KD - 1)
                linear(L["q"], ada=None if last else "q")

                def pre_square(t):
                    i = NORM_TILES.index(t)
                    Tn = T2 if t == KB else TQ
                    act.wait_ge(acc_free.sem, acc_free.at(L["kv"]["g0"] + taken_with(t)))
                    if i >= 2:
                        act.wait_ge(A["normed"].sem, A["normed"].at(i - 1))
                    nc.scalar.activation(tmp_b[:, i % 2, 0:Tn], proj2[:, t, 0:Tn], ACT.Square).then_inc(A["pre_sq"].sem, 1)

                def pre_work(i):
                    if i == 0:
                        pre_square(3)
                        pre_square(4)
                    for x in PRE.get(i, []):
                        what, t = x
                        if what == "rope":
                            continue
                        act.wait_ge(A["pre_pe"].sem, A["pre_pe"].at(PRE_ORDER.index(x) + 1))
                        if what == "norm":
                            Tn = T2 if t == KB else TQ
                            ins = nc.scalar.activation(tmp_b[:, NORM_TILES.index(t) % 2, 0:Tn], ps[:, pre_bank(x), 0:Tn],
                                                       ACT.Sqrt, bias=eps)
                        else:
                            ins = nc.scalar.copy(vt[:, V_TILES.index(t), :, :],
                                                 ps[:, pre_bank(x), :].rearrange("p (t d) -> p t d", t=4))
                        ins.then_inc(A["pre_act"].sem, 1)
                    if i == 1:
                        pre_square(KB)

                linear(L["kv"], behind=pre_work)
                act.wait_ge(A["roped"].sem, A["roped"].at(7))
                for w, t in ((0, KA), (1, KB)):
                    nc.scalar.copy(k_sw[0:HD, w, :], proj2[HD:P, t, :])
                    ins = nc.scalar.copy(k_sw[HD:P, w, :], proj2[0:HD, t, :])
                ins.then_inc(A["k_sw"].sem, 1)
                pre_work(5)

                def exps(i):
                    n, q0, k0, nk = A["items"][i]
                    x = i % 2
                    act.wait_ge(A["logits"].sem, A["logits"].at(i + 1))
                    for q in range(2):
                        src = s[:, x, q, 0:nk] if kind(n) != "B" and q0 == 0 else scores_of(i)[:, q, :]
                        scale = 1.0 if kind(n) != "B" and q0 == 0 else HD ** -0.5
                        ins = nc.scalar.activation(s[:, x, q, 0:nk], src, ACT.Exp, scale=scale,
                                                   bias=st[:, x, q:q + 1], accum_out=st[:, x, 2 + q:3 + q])
                    if kind(n) == "A":
                        ins = nc.scalar.activation(st[:, x, 4:6], st[:, x, 0:2], ACT.Exp, bias=sink[:, n:n + 1])
                    ins.then_inc(A["exped"].sem, 1)

                def outs(i):
                    n, q0, k0, nk = A["items"][i]
                    x = i % 2
                    act.wait_ge(A["turned"].sem, A["turned"].at(i + 1))
                    kts = nk // P
                    nc.scalar.copy(pT[:, x, 0:kts, :], ps[:, 4:6, :].rearrange("p b (t q) -> p (b t) q", t=2)[:, 0:kts, :]).then_inc(A["pt"].sem, 1)

                def yhi(i):
                    n, q0, k0, nk = A["items"][i]
                    off = HD * (n % 2)
                    act.wait_ge(A["o"].sem, A["o"].at(i + 1))
                    nc.scalar.copy(u_hi[off:off + HD, n // 2, q0:q0 + 256], ps[off:off + HD, 6 + i % 2, 0:256]).then_inc(A["yhi"].sem, 1)

                def scores_of(i):
                    nk = A["items"][i][3]
                    return ps[:, 2 * (i % 2):2 * (i % 2) + 2, 0:nk]

                N = len(A["items"])
                for i in range(N + 2):
                    if i < N:
                        exps(i)
                    if 1 <= i <= N:
                        outs(i - 1)
                    if i >= 2:
                        yhi(i - 2)
                linear(L["out"], (f"l{l}c", h2, TQ), ada=None if last else "out")
                modulated(f"l{l}c", L["out"], l, 6, TQ, KD - 2)
                ffn_up(L["f2a"], L["sig"][1], TQ, FFN_F, hf_hi, 1, None if last else "f2a")
                ffn_down(L["f2b"], 1, None if last else "f2b", ("end2", h2, SEQ) if last else ("l1a", h2, T2))
            fin = VEC["final2"][0]
            norm("end2", end_of(layers[1]["f2b"]), h2, SEQ, scale=lambda k, q: vec[:, fin + k:fin + k + 1], dest=h2, splits=((0, SEQ),),
                 rows_squared=KD - 1)

        @block.vector
        def _(dve):
            chain = [0]

            def link(ins):
                chain[0] += 1
                ins.then_inc(dve_chain.sem, 1)
                dve.wait_ge(dve_chain.sem, chain[0])

            tt, ts, stt = nc.vector.tensor_tensor, nc.vector.tensor_scalar, nc.vector.scalar_tensor_tensor

            def split_lo(u, slot, elems):
                dve.wait_ge(hi_done.sem, u + 1)
                tt(w_lo[:, slot, 0:elems], raw[:, slot, 0:elems], w_hi[:, slot, 0:elems].bitcast(F32),
                   ALU.subtract).then_inc(lo_done.sem, 1)

            def next_lo(stg, i, j, per=4):
                u = stg["u0"] + per * i + j + 2
                slot = (stg["u0"] + j) % 2
                if isinstance(u, int):
                    if u < N_UNITS:
                        split_lo(u, slot, elems_of[u])
                else:
                    split_lo(u, slot, stg["elems"])

            def ada_quarter(j, quarter):
                slot = quarter % 2
                dve.wait_ge(ada_full[slot], 32 * j + 16 * (quarter // 2) + 16)
                for kk in range(2):
                    k = 2 * quarter + kk
                    for v in range(2):
                        if k == 0:
                            if v == 0:
                                need(dve, ada_sum, j)
                            ins = ts(ada_acc[:, v, :], ada_w[:, slot, kk, :], sc_c[:, k, v:v + 1], None, ALU.mult)
                        else:
                            dve.wait_ge(ada_mac.sem, 16 * j + 2 * k + v - 1)
                            ins = stt(out=ada_acc[:, v, :], in0=ada_w[:, slot, kk, :], scalar=sc_c[:, k, v:v + 1],
                                      in1=ada_acc[:, v, :], op0=ALU.mult, op1=ALU.add)
                        ins.then_inc(ada_mac.sem, 1)

            def ada_out(j):
                dve.wait_ge(ada_sum.sem, j + 1)
                nj = ADA_COLS // P
                v = bass.ds(nj * j, nj)
                tt(mod[:, v, :], ps[:, 4, 0:2 * nj].rearrange("p (t v) -> p t v", v=2), b_ada[:, v, :],
                   ALU.add).then_inc(mod_done.sem, 1)

            def norm(nm, h, T, first=0, split=True):
                n = norm_of[nm]
                dve.wait_ge(n["root"].sem, n["root"].at(1))
                nc.vector.reciprocal(rstd[:, 0:T], rstd[:, 0:T]).then_inc(n["rstd"].sem, 1)
                dve.wait_ge(n["rstd"].sem, n["rstd"].at(1))

                def t_row(k):
                    if k >= 2:
                        dve.wait_ge(n["w"].sem, n["w"].at(k - 1))
                    tt(tmp_a[:, k % 2, 0:T], h[:, k, first:first + T], rstd[:, 0:T], ALU.mult).then_inc(n["t"].sem, 1)

                t_row(0)
                for k in range(KD):
                    if k + 1 < KD:
                        t_row(k + 1)
                    if split:
                        dve.wait_ge(n["w"].sem, n["w"].at(k + 1))
                        nc.vector.tensor_copy(u_hi[:, k, 0:T], tmp_b[:, k % 2, 0:T]).then_inc(n["hi"].sem, 1)

            def ffn_up(stg, sig, T, n_units, ada, weighted=False):
                first, per = ADA[ada] if ada else (0, 0)
                plan = ada_plan(per)

                def step(i, j, work):
                    n = 4 * i + j
                    g = stg["g0"] + j
                    if work and plan[j][1] is not None:
                        c = first + per * i + plan[j][1]
                        if not (isinstance(c, int) and c < first):
                            ada_out(c)
                    dve.wait_ge(sig["silu"].sem, sig["silu"].at(n + 1))
                    if weighted:
                        e = 2 * i + j // 2
                        ce = comb[:, e, :] if isinstance(e, int) else comb[:, bass.ds(e, 1), :].rearrange("p o t -> p (o t)")
                        tt(tmp_a[:, j % 2, 0:T], tmp_a[:, j % 2, 0:T], ce, ALU.mult).then_inc(sig["comb"].sem, 1)
                        dve.wait_ge(sig["comb"].sem, sig["comb"].at(n + 1))
                    need(dve, sig["lo"], n - 1)
                    tt(tmp_b[:, j % 2, 0:T], tmp_a[:, j % 2, 0:T], ps[:, 2 * (g % 2) + 1, 0:T], ALU.mult).then_inc(acc_free.sem, 1)
                    next_lo(stg, i, j)
                    if work:
                        for c, quarter in plan[j][0]:
                            ada_quarter(first + per * i + c, quarter)

                def body(i):
                    for j in range(4):
                        step(i, j, True)
                nb = n_units // 4
                repeat(dve, nb, body)
                if ada and n_units % 4 == 0:
                    ada_out(first + per * nb - 1)
                for j in range(n_units % 4):
                    step(nb, j, False)
                    if j == 0 and ada:
                        ada_out(first + per * nb - 1)

            def ffn_down(stg, add, ada):
                first, per = ADA[ada] if ada else (0, 0)
                plan = ada_plan(per)

                def body(i):
                    for j in range(4):
                        if plan[j][1] is not None:
                            c = first + per * i + plan[j][1]
                            if not (isinstance(c, int) and c < first):
                                ada_out(c)
                        if j % 2:
                            m = 2 * i + j // 2
                            dve.wait_ge(unit_done.sem, stg["u0"] + 4 * i + j + 1)
                            add(m, ps[:, 2 * ((stg["g0"] + j // 2) % 2), :]).then_inc(acc_free.sem, 1)
                        for c, quarter in plan[j][0]:
                            ada_quarter(first + per * i + c, quarter)
                        next_lo(stg, i, j)
                repeat(dve, 4, body)
                if ada:
                    ada_out(first + per * 4 - 1)

            def add_plain(m, acc):
                return tt(row(h1, m, 0, T1), acc[:, 0:T1], row(h1, m, 0, T1), ALU.add)

            def add_gated(T):
                def add(m, acc):
                    for v in range(T // SEQ):
                        c0 = SEQ * v
                        g = gate[:, m, v:v + 1] if isinstance(m, int) else gate[:, bass.ds(m, 1), v:v + 1].rearrange("p o t -> p (o t)")
                        ins = stt(out=row(h2, m, c0, c0 + SEQ), in0=acc[:, c0:c0 + SEQ], scalar=g,
                                  in1=row(h2, m, c0, c0 + SEQ), op0=ALU.mult, op1=ALU.add)
                    return ins
                return add

            def linear(stg, take, ada=None, tail=None, behind=None):
                for i in range(stg["units"]):
                    if i == 0 and tail is not None:
                        ada_out(tail)
                    work, complete = ada_of_unit(ada, i)
                    if complete is not None:
                        ada_out(complete)
                    u, g = stg["u0"] + i, stg["g0"] + i
                    dve.wait_ge(unit_done.sem, u + 1)
                    take(i, ps[:, 2 * (g % 2):2 * (g % 2) + 2, :]).then_inc(acc_free.sem, 1)
                    for c, quarter in work:
                        ada_quarter(c, quarter)
                    if u + 2 < N_UNITS:
                        split_lo(u + 2, u % 2, elems_of[u + 2])
                    if behind:
                        behind(i)

            dve.wait_ge(turned.sem, turned.at(1))
            nc.vector.tensor_copy(vec[:, :], ps[:, 0, 0:VEC_ROWS]).then_inc(rows_out.sem, 1)
            dve.wait_ge(turned.sem, turned.at(2))
            nc.vector.tensor_copy(h1[:, :, 0:N_META], ps[:, 1, 0:128].rearrange("p (k t) -> p k t", k=KD)
                                  ).then_inc(rows_out.sem, 1)
            for b in range(4):
                dve.wait_ge(turned.sem, turned.at(3 + min(b, 2)))
                ins = nc.vector.tensor_copy(h1[:, 2 * b:2 * b + 2, N_META:T1], ps[:, 2 + b, :].rearrange("p (k t) -> p k t", k=2))
                if b != 2:
                    ins.then_inc(rows_out.sem, 1)
            for t in range(4):
                dve.wait_ge(turned.sem, turned.at(6 + t))
                nc.vector.tensor_copy(h2[:, 2 * t:2 * t + 2, SEQ:T2], ps[:, 6 + t % 2, :].rearrange("p (k t) -> p k t", k=2)).then_inc(rows_out.sem, 1)
            dve.wait_ge(turned.sem, turned.at(10))
            for v in range(2):
                for l in range(2):
                    ins = nc.vector.tensor_copy(b_ada[:, 72 * l:72 * l + 72, v], ps[:, 0, 72 * l:72 * l + 72])
            ins.then_inc(rows_out.sem, 3)
            split_lo(0, 0, UNIT)
            split_lo(1, 1, UNIT)
            norm("mix1", h1, T1)

            def to_proj1(i, acc):
                if i == 0:
                    dve.wait_ge(rows_out.sem, rows_out.at(12))
                return nc.vector.tensor_copy(proj1[:, 2 * i:2 * i + 2, :], acc[:, :, 0:T1])
            linear(st_in1, to_proj1, "in1")

            dve.wait_ge(ld_small, 64)
            link(nc.vector.tensor_copy(glr_hi[:, :, :], glr_raw[:, :, :]))
            tt(glr_lo[:, :, :], glr_raw[:, :, :], glr_hi[:, :, :].bitcast(F32), ALU.subtract).then_inc(ev["low_split"], 1)
            dve.wait_ge(ev["win_zero"], 1)
            link(nc.vector.tensor_copy(win_a[:, :, PAD:PAD + T1], proj1[:, 0:4, :]))
            n = PAD + T1
            link(tt(win_b[:, :, 1:n], win_a[:, :, 1:n], win_a[:, :, 0:n - 1], ALU.add))
            link(tt(win_a[:, 1:4, 3:n], win_b[:, 1:4, 3:n], win_b[:, 1:4, 1:n - 2], ALU.add))
            link(tt(win_b[:, 2:4, 7:n], win_a[:, 2:4, 7:n], win_a[:, 2:4, 3:n - 4], ALU.add))
            link(tt(win_a[:, 3:4, 15:n], win_b[:, 3:4, 15:n], win_b[:, 3:4, 7:n - 8], ALU.add))
            for g, w in enumerate((win_b, win_a, win_b, win_a)):
                ins = tt(w[:, g, PAD:n], w[:, g, PAD:n], cnt[:, g, :], ALU.mult)
            link(ins)
            for g, w in enumerate((win_b, win_a, win_b, win_a)):
                ins = tt(w[:, g, PAD:n], w[:, g, PAD:n], proj1[:, g, :], ALU.subtract)
            ins.then_inc(ev["windows"], 1)
            dve.wait_ge(ev["low_sum"], 1)
            nc.vector.tensor_copy(glr[:, :], ps[:, 4, 0:T1]).then_inc(ev["low_out"], 1)
            dve.wait_ge(ev["z_ln"], 1)
            bg = VEC["b_gate"][0]
            for t in range(2):
                ins = ts(lgb[:, t, :], ps[:, 4 + t, 0:T1], vec[:, bg + t:bg + t + 1], 0.0, ALU.add, ALU.min)
            link(ins)
            link(tt(lga[:, :, :], lgb[:, :, :], lga[:, :, :], ALU.subtract))
            link(ts(lga[:, :, :], lga[:, :, :], 1.0 / 16.0, None, ALU.mult))
            for t in range(2):
                for c0, L in CHUNKS:
                    ins = nc.vector.tensor_tensor_scan(lgb[:, t, c0:c0 + L], one.to_broadcast([P, L]),
                                                       lga[:, t, c0:c0 + L], 0.0, ALU.mult, ALU.add)
            ins.then_inc(ev["b_sum"], 1)
            dve.wait_ge(ev["exps"], 1)
            for h in range(4):
                o, t = HD * (h % 2), h // 2
                stt(out=qz[o:o + HD, h, :], in0=proj1[o:o + HD, 4 + t, :], scalar=HD ** -0.5, in1=lga[o:o + HD, t, :],
                    op0=ALU.mult, op1=ALU.mult)
            tt(kend[:, :, :], kend[:, :, :], proj1[:, 6:8, :], ALU.mult)
            tt(kt[:, :, :], kt[:, :, :], proj1[:, 6:8, :], ALU.mult).then_inc(ev["keys"], 1)
            dve.wait_ge(ev["pooled_sum"], 4)
            sc0 = VEC["pool_scale"][0]
            for g in range(4):
                if g:
                    dve.wait_ge(ev["pooled_out"], g)
                link(ts(tmp_a[:, 0, 0:T1], ps[:, 4 + g, 0:T1], vec[:, sc0 + g:sc0 + g + 1], None, ALU.mult))
                link(nc.vector.tensor_copy(u_hi[:, g, 0:T1], tmp_a[:, 0, 0:T1]))
                tt(u_lo[:, g, 0:T1], tmp_a[:, 0, 0:T1], u_hi[:, g, 0:T1].bitcast(F32),
                   ALU.subtract).then_inc(ev["pooled_out"], 1)
            for n, (c0, L) in enumerate(CHUNKS):
                dve.wait_ge(ev["scores"], n + 1)
                if n >= 2:
                    dve.wait_ge(ev["o_sum"], n - 1)
                nc.vector.tensor_copy(sT[0:L, n % 2, :, 0:L],
                                      ps[0:L, 6, 0:256].rearrange("p (h c) -> p h c", h=4)[:, :, 0:L]
                                      ).then_inc(ev["scores_out"], 1)
                dve.wait_ge(ev["o_sum"], n + 1)
                nc.vector.tensor_copy(oT[:, :, c0:c0 + L], ps[:, 7, 0:256].rearrange("p (h c) -> p h c", h=4)
                                      [:, :, 0:L]).then_inc(ev["o_out"], 1)
                if n == len(CHUNKS) - 1:
                    break
                dve.wait_ge(ev["chunk_state"], n + 1)
                if n:
                    dve.wait_ge(ev["state"], n)
                d = ps[:, 4 + n % 2, :].rearrange("p (h v) -> p h v", h=4)
                if n == 0:
                    ins = nc.vector.tensor_copy(S[:, :, :], d)
                else:
                    for h in range(4):
                        ins = stt(out=S[:, h, :], in0=S[:, h, :], scalar=lga[:, h // 2, c0 + L - 1:c0 + L], in1=d[:, h, :],
                                  op0=ALU.mult, op1=ALU.add)
                ins.then_inc(ev["state"], 1)
            dve.wait_ge(ev["silu_r"], 1)
            dve.wait_ge(ev["o_out"], len(CHUNKS))
            gw = VEC["gla_norm"][0]
            stt(out=proj1[:, 12:16, :], in0=oT[:, :, :], scalar=vec[:, gw:gw + 1], in1=proj1[:, 12:16, :], op0=ALU.mult,
                op1=ALU.mult).then_inc(ev["gated"], 1)
            dve.wait_ge(ev["gated"], 1)
            for h in range(4):
                dve.wait_ge(ev["o_root"], h + 1)
                link(nc.vector.reciprocal(proj1[:, 4 + h, :], proj1[:, 4 + h, :]))
                tt(oT[:, h, :], proj1[:, 12 + h, :], proj1[:, 4 + h, :], ALU.mult).then_inc(ev["gla_out"], 1)

            def add_h1(i, acc):
                return tt(h1[:, 2 * i:2 * i + 2, :], acc[:, :, 0:T1], h1[:, 2 * i:2 * i + 2, :], ALU.add)
            linear(st_out1, add_h1)

            norm("ffn1", h1, T1)
            dve.wait_ge(ld_router, 64)
            link(nc.vector.tensor_copy(wr_hi[:, :, :], wr[:, :, :]))
            tt(wr_lo[:, :, :], wr[:, :, :], wr_hi[:, :, :].bitcast(F32), ALU.subtract).then_inc(ev["r_split"], 1)
            dve.wait_ge(ev["logits"], 1)
            nc.vector.tensor_copy(lgT[:, :], ps[0:20, 6, 0:T1]).then_inc(ev["logits_out"], 1)
            dve.wait_ge(ev["logits_turned"], 1)
            for t in range(3):
                ins = tt(lg[:, t, :], ps[:, 7, 20 * t:20 * t + 20], rb[:, :], ALU.add)
            link(ins)

            def spread(v, n=4):
                return v.rearrange("p (t o) -> p t o", o=1).to_broadcast([P, 3, n])

            ranks = rank.rearrange("p (o k) -> p o k", o=1).to_broadcast([P, 3, 4])

            def first_of(dst, v, top, scratch, m):
                link(tt(scratch[:, :, :], v, spread(top), ALU.is_equal))
                link(tt(scratch[:, :, :], scratch[:, :, :], ranks, ALU.mult))
                link(nc.vector.reduce_max(m[:, :], scratch[:, :, :], AX_X))
                link(tt(dst, scratch[:, :, :], spread(m[:, :]), ALU.is_equal))

            link(nc.vector.reduce_max(r1a[:, :], lg[:, :, 0:4], AX_X))
            tt(r4a[:, :, :], lg[:, :, 0:4], spread(r1a[:, :]), ALU.subtract).then_inc(ev["g_shift"], 1)
            first_of(oh_g[:, :, :], lg[:, :, 0:4], r1a[:, :], r4c, r1b)
            link(tt(r16[:, :, :].rearrange("p t (g k) -> p t g k", g=4), lg[:, :, 4:20].rearrange("p t (g k) -> p t g k", g=4),
                    oh_g[:, :, :].rearrange("p t (g o) -> p t g o", o=1).to_broadcast([P, 3, 4, 4]), ALU.mult))
            link(nc.vector.reduce_sum(r4c[:, :, :], r16[:, :, :].rearrange("p t (g k) -> p t k g", g=4), AX_X))
            link(nc.vector.reduce_max(r1b[:, :], r4c[:, :, :], AX_X))
            tt(r4c[:, :, :], r4c[:, :, :], spread(r1b[:, :]), ALU.subtract).then_inc(ev["e_shift"], 1)
            dve.wait_ge(ev["g_exp"], 1)
            link(nc.vector.reduce_sum(pg[:, :], r4b[:, :, :], AX_X))
            link(nc.vector.reciprocal(pg[:, :], pg[:, :]))
            dve.wait_ge(ev["e_exp"], 1)
            link(nc.vector.reduce_sum(r1a[:, :], prob[:, :, :], AX_X))
            link(nc.vector.reciprocal(r1a[:, :], r1a[:, :]))
            link(tt(prob[:, :, :], prob[:, :, :], spread(r1a[:, :]), ALU.mult))
            link(nc.vector.reduce_max(r1a[:, :], prob[:, :, :], AX_X))
            first_of(oh1[:, :, :], prob[:, :, :], r1a[:, :], r4c, r1b)
            link(stt(out=r4b[:, :, :], in0=oh1[:, :, :], scalar=-2.0, in1=prob[:, :, :], op0=ALU.mult, op1=ALU.add))
            link(nc.vector.reduce_max(r1c[:, :], r4b[:, :, :], AX_X))
            first_of(r4a[:, :, :], r4b[:, :, :], r1c[:, :], r4c, r1b)
            link(tt(r4a[:, :, :], r4a[:, :, :], oh1[:, :, :], ALU.add))
            link(tt(r1a[:, :], r1a[:, :], r1c[:, :], ALU.add))
            link(nc.vector.reciprocal(r1a[:, :], r1a[:, :]))
            link(tt(r1a[:, :], r1a[:, :], pg[:, :], ALU.mult))
            link(tt(r4a[:, :, :], r4a[:, :, :], prob[:, :, :], ALU.mult))
            link(tt(r4a[:, :, :], r4a[:, :, :], spread(r1a[:, :]), ALU.mult))
            for t in range(3):
                ins = tt(r16[:, t, :].rearrange("p (g k) -> p g k", g=4),
                         oh_g[:, t, :].rearrange("p (g o) -> p g o", o=1).to_broadcast([P, 4, 4]),
                         r4a[:, t, :].rearrange("p (o k) -> p o k", o=1).to_broadcast([P, 4, 4]), ALU.mult)
            ins.then_inc(ev["shares"], 1)
            dve.wait_ge(ev["shares_turned"], 1)
            nc.vector.tensor_copy(combT[:, 0:256], ps[0:16, 7, 0:256])
            link(nc.vector.tensor_copy(combT[:, 256:272], ps[0:16, 7, 256 + 112:384]))
            nc.vector.tensor_copy(pick[:, :], ident[0:16, 0:16])
            link(nc.vector.tensor_copy(comb_hi[:, :], combT[:, :]))
            tt(comb_lo[:, :], combT[:, :], comb_hi[:, :].bitcast(F32), ALU.subtract).then_inc(ev["shares_out"], 1)
            for e in range(1, N_EXPERTS, 2):
                dve.wait_ge(ev["share_sum"], e + 1)
                nc.vector.tensor_copy(comb[:, e, :], ps[:, 4 + e % 4, 0:T1]).then_inc(ev["share_out_odd"], 1)
            dve.wait_ge(ev["share_out"], N_EXPERTS // 2)
            dve.wait_ge(ev["share_out_odd"], N_EXPERTS // 2)
            ffn_up(st_moe_a, moe_sig, T1, MOE_F, None, weighted=True)
            ffn_down(st_moe_b, add_plain, "moe_b")
            norm("end1", h1, SEQ, first=N_META, split=False)
            def modulation(l, nw, m, after):
                t0 = 72 * l + 8 * m
                w0 = VEC[nw][0] + 8 * l
                dve.wait_ge(acc_free.sem, acc_free.at(end_of(after)))
                need(dve, mod_done, {0: 4, 3: 10, 6: 16}[m] + ADA_CHUNKS * l)
                for v in range(2):
                    ins = stt(out=coef[:, :, v], in0=mod[:, t0 + 8:t0 + 16, v], scalar=1.0, in1=vec[:, w0:w0 + 8],
                              op0=ALU.add, op1=ALU.mult)
                link(ins)

            def gates(l, m, by):
                t0 = 72 * l + 8 * m + 16
                need(dve, mod_done, {0: 6, 3: 12, 6: 18}[m] + ADA_CHUNKS * l)
                link(ts(gate[:, :, :], mod[:, t0:t0 + 8, :], by, None, ALU.mult))

            for l in range(2):
                L, A = layers[l], attn[l]
                last = l == 1
                TQ = SEQ if last else T2
                modulation(l, "ffn1", 0, layers[0]["f2b"] if last else st_moe_b)
                norm(f"l{l}a", h2, T2)
                ffn_up(L["f1a"], L["sig"][0], T2, FFN_F, "l1_f1a" if last else "f1a")
                gates(l, 0, 0.5)
                ffn_down(L["f1b"], add_gated(T2), None if last else "f1b")
                modulation(l, "mix", 3, L["f1b"])
                norm(f"l{l}b", h2, T2)
                gates(l, 3, 1.0)
                linear(L["q"], lambda i, acc: nc.vector.tensor_copy(proj2[:, 2 * i:2 * i + 2, 0:TQ], acc[:, :, 0:TQ]),
                       None if last else "q")

                def pre_work(i):
                    for x in PRE.get(i, []):
                        what, t = x
                        n = PRE_ORDER.index(x)
                        if what == "norm":
                            k = NORM_TILES.index(t)
                            Tn = T2 if t == KB else TQ
                            dve.wait_ge(A["pre_act"].sem, A["pre_act"].at(pre_count(("norm", "value"), n + 1)))
                            nc.vector.reciprocal(tmp_b[:, k % 2, 0:Tn], tmp_b[:, k % 2, 0:Tn]).then_inc(A["pre_inv"].sem, 1)
                            dve.wait_ge(A["pre_inv"].sem, A["pre_inv"].at(k + 1))
                            w0 = VEC["k_norm" if t == KB else "q_norm"][0] + l
                            stt(out=proj2[:, t, 0:Tn], in0=proj2[:, t, 0:Tn], scalar=vec[:, w0:w0 + 1],
                                in1=tmp_b[:, k % 2, 0:Tn], op0=ALU.mult, op1=ALU.mult).then_inc(A["normed"].sem, 1)
                        elif what == "rope":
                            dve.wait_ge(A["pre_pe"].sem, A["pre_pe"].at(n + 1))
                            tt(tmp_a[:, 0, 0:SEQ], proj2[:, t, 0:SEQ], cos, ALU.mult)
                            tt(tmp_a[:, 1, 0:SEQ], ps[:, pre_bank(x), 0:SEQ], sin, ALU.mult).then_inc(A["rot"].sem, 1)
                            dve.wait_ge(A["rot"].sem, A["rot"].at(pre_count(("rope",), n + 1)))
                            tt(proj2[:, t, 0:SEQ], tmp_a[:, 0, 0:SEQ], tmp_a[:, 1, 0:SEQ], ALU.add).then_inc(A["roped"].sem, 1)
                            dve.wait_ge(A["roped"].sem, A["roped"].at(pre_count(("rope",), n + 1)))

                linear(L["kv"], lambda i, acc: nc.vector.tensor_copy(proj2[:, 8 + 2 * i:10 + 2 * i, :], acc),
                       tail=None if last else 15, behind=pre_work)
                for i in range(6):
                    dve.wait_ge(A["bias"].sem, A["bias"].at(i + 1))
                    tt(bias_c[:, i // 3, 2 * (i % 3):2 * (i % 3) + 2, :],
                       ps[:, BIAS_BANKS[i], :].rearrange("p (h k) -> p h k", h=2),
                       nbr_mask.rearrange("p (o k) -> p o k", o=1).to_broadcast([P, 2, SEQ]),
                       ALU.add).then_inc(A["bias_out"].sem, 1)
                dve.wait_ge(A["bias_out"].sem, A["bias_out"].at(6))
                def scores_of(i):
                    nk = A["items"][i][3]
                    return ps[:, 2 * (i % 2):2 * (i % 2) + 2, 0:nk]

                def logits(i):
                    n, q0, k0, nk = A["items"][i]
                    x = i % 2
                    dve.wait_ge(A["scores"].sem, A["scores"].at(i + 1))
                    if i >= 2:
                        dve.wait_ge(A["turned"].sem, A["turned"].at(i - 1))
                    sc = scores_of(i)
                    c = HD ** -0.5
                    masked = kind(n) != "B" and q0 == 0
                    if kind(n) == "A" and q0 == 0:
                        link(stt(out=s[:, x, :, :], in0=sc, scalar=c, in1=win_mask, op0=ALU.mult, op1=ALU.add))
                    elif kind(n) == "C" and q0 == 0:
                        stt(out=s[:, x, :, 0:SEQ], in0=sc[:, :, 0:SEQ], scalar=c,
                            in1=bias_c[:, :, n - A_HEADS - B_HEADS, :], op0=ALU.mult, op1=ALU.add)
                        link(ts(s[:, x, :, SEQ:T2], sc[:, :, SEQ:T2], c, None, ALU.mult))
                    src = s[:, x, :, :] if masked else sc
                    link(nc.vector.reduce_max(st[:, x, 0:2], src, AX_X))
                    if kind(n) == "A":
                        link(ts(st[:, x, 0:2], st[:, x, 0:2], 1.0 if masked else c, sink[:, n:n + 1], ALU.mult, ALU.max))
                        ts(st[:, x, 0:2], st[:, x, 0:2], -1.0, None, ALU.mult).then_inc(A["logits"].sem, 1)
                    else:
                        ts(st[:, x, 0:2], st[:, x, 0:2], -1.0 if masked else -c, None, ALU.mult).then_inc(A["logits"].sem, 1)

                def normal(i):
                    n, q0, k0, nk = A["items"][i]
                    x = i % 2
                    dve.wait_ge(A["exped"].sem, A["exped"].at(i + 1))
                    if kind(n) == "A":
                        link(tt(st[:, x, 2:4], st[:, x, 2:4], st[:, x, 4:6], ALU.add))
                    link(nc.vector.reciprocal(st[:, x, 6:8], st[:, x, 2:4]))
                    for q in range(2):
                        ins = ts(s[:, x, q, 0:nk], s[:, x, q, 0:nk], st[:, x, 6 + q:7 + q], None, ALU.mult)
                    ins.then_inc(A["probs"].sem, 1)

                def ylo(i):
                    n, q0, k0, nk = A["items"][i]
                    off = HD * (n % 2)
                    dve.wait_ge(A["yhi"].sem, A["yhi"].at(i + 1))
                    tt(u_lo[off:off + HD, n // 2, q0:q0 + 256], ps[off:off + HD, 6 + i % 2, 0:256],
                       u_hi[off:off + HD, n // 2, q0:q0 + 256].bitcast(F32), ALU.subtract).then_inc(A["ylo"].sem, 1)

                N = len(A["items"])
                logits(0)
                for i in range(N + 2):
                    if i < N:
                        normal(i)
                    if i + 1 < N:
                        logits(i + 1)
                    if i >= 2:
                        ylo(i - 2)

                def add_h2(i, acc):
                    for t in range(2):
                        for v in range(TQ // SEQ):
                            m, c0 = 2 * i + t, SEQ * v
                            ins = stt(out=h2[:, m, c0:c0 + SEQ], in0=acc[:, t, c0:c0 + SEQ], scalar=gate[:, m, v:v + 1],
                                      in1=h2[:, m, c0:c0 + SEQ], op0=ALU.mult, op1=ALU.add)
                    return ins
                linear(L["out"], add_h2, None if last else "out")
                modulation(l, "ffn2", 6, L["out"])
                norm(f"l{l}c", h2, TQ)
                ffn_up(L["f2a"], L["sig"][1], TQ, FFN_F, None if last else "f2a")
                gates(l, 6, 0.5)
                ffn_down(L["f2b"], add_gated(TQ), None if last else "f2b")
            norm("end2", h2, SEQ, split=False)
            for t in range(4):
                dve.wait_ge(turned.sem, turned.at(10 + t + 1))
                nc.vector.tensor_copy(o_rows[:, t // 2, 512 * (t % 2):512 * (t % 2) + 512], ps[:, 2 + t, :]).then_inc(rows_out.sem, 1)

        @block.gpsimd
        def _(pool):
            chain = [0]

            def link(ins):
                chain[0] += 1
                ins.then_inc(pool_chain.sem, 1)
                pool.wait_ge(pool_chain.sem, chain[0])

            tt = nc.gpsimd.tensor_tensor

            def norm(nm, T):
                n = norm_of[nm]
                for k in range(KD):
                    pool.wait_ge(n["hi"].sem, n["hi"].at(k + 1))
                    tt(u_lo[:, k, 0:T], tmp_b[:, k % 2, 0:T], u_hi[:, k, 0:T].bitcast(F32), ALU.subtract).then_inc(n["lo"].sem, 1)

            def ffn_up(sig, T, n_units, hi, lo):
                def step(i, j):
                    n = 4 * i + j
                    pool.wait_ge(sig["hi"].sem, sig["hi"].at(n + 1))
                    r = [x[:, n, 0:T] if isinstance(n, int) else x[:, bass.ds(n, 1), 0:T].rearrange("p o t -> p (o t)") for x in (hi, lo)]
                    tt(r[1], tmp_b[:, j % 2, 0:T], r[0].bitcast(F32), ALU.subtract).then_inc(sig["lo"].sem, 1)

                def body(i):
                    for j in range(4):
                        step(i, j)
                repeat(pool, n_units // 4, body)
                for j in range(n_units % 4):
                    step(n_units // 4, j)

            pool.wait_ge(rows_out.sem, rows_out.at(12))
            nc.gpsimd.memset(glr_raw[:, :, :], 0.0).then_inc(ev["low_zero"], 1)
            nc.gpsimd.memset(qz[:, :, :], 0.0)
            norm("mix1", T1)
            nc.gpsimd.memset(win_a[:, :, 0:PAD], 0.0).then_inc(ev["win_zero"], 1)
            for n, (c0, L) in enumerate(CHUNKS):
                pool.wait_ge(ev["scores_out"], n + 1)
                nc.gpsimd.affine_select(out=sT[0:L, n % 2, :, 0:L], in_=sT[0:L, n % 2, :, 0:L], compare_op=ALU.is_ge, fill=0.0,
                                        base=0, pattern=[[0, 4], [1, L]], channel_multiplier=-1).then_inc(ev["causal"], 1)
            for h in range(4):
                pool.wait_ge(ev["gla_hi"], h + 1)
                tt(u_lo[:, 4 + h, 0:T1], oT[:, h, :], u_hi[:, 4 + h, 0:T1].bitcast(F32),
                   ALU.subtract).then_inc(y_ready[0].sem, 5 if h == 0 else 1)
            norm("ffn1", T1)
            ffn_up(moe_sig, T1, MOE_F, hm_hi, hm_lo)
            for l in range(2):
                TQ = SEQ if l == 1 else T2
                norm(f"l{l}a", T2)
                ffn_up(layers[l]["sig"][0], T2, FFN_F, hf_hi, hf_lo)
                norm(f"l{l}b", T2)
                norm(f"l{l}c", TQ)
                ffn_up(layers[l]["sig"][1], TQ, FFN_F, hf_hi, hf_lo)

        @block.tensor
        def _(pe):
            mm = nc.tensor.matmul

            def turn(dst, src, n):
                return nc.tensor.transpose(dst, src, ident[0:n, 0:n])

            def products(acc, slot, cols, moving, T, first, last):
                n = len(moving)
                for i, (c, (m_hi, m_lo)) in enumerate(zip(cols, moving)):
                    w1, w2 = w_hi[:, slot, c:c + P], w_lo[:, slot, c:c + P]
                    mm(acc, w1, m_hi, start=(first and i == 0), stop=False)
                    mm(acc, w1, m_lo, start=False, stop=False)
                    ins = mm(acc, w2, m_hi, start=False, stop=(last and i == n - 1))
                return ins

            def rows_of(hi, lo, k0, n, T):
                return [(hi[:, k, 0:T], lo[:, k, 0:T]) for k in range(k0, k0 + n)]

            def begin(u, g):
                pe.wait_ge(lo_done.sem, u + 1)
                if g is not None:
                    need(pe, acc_free, g - 1)

            def mean_square(nm, k, slot, T, start, stop):
                n = norm_of[nm]
                pe.wait_ge(n["sq"].sem, n["sq"].at(k + 1))
                mm(ps[:, 5, 0:T], ones_d, tmp_b[:, slot, 0:T], start=start, stop=stop).then_inc(n["ms"].sem, 1)

            def norm(nm, T, k0=0):
                for k in range(k0, KD):
                    mean_square(nm, k, k % 2, T, k == 0, k == KD - 1)

            def two_tiles(u, g, cols, T, ready=None):
                slot = u % 2
                if ready is None:
                    for t in range(2):
                        ins = products(ps[:, 2 * g + t, 0:T], slot, [cols(t, k) for k in range(KD)],
                                       rows_of(u_hi, u_lo, 0, KD, T), T, True, True)
                else:
                    for k in range(KD):
                        pe.wait_ge(ready.sem, ready.at(k + 1))
                        for t in range(2):
                            ins = products(ps[:, 2 * g + t, 0:T], slot, [cols(t, k)], rows_of(u_hi, u_lo, k, 1, T), T,
                                           k == 0, k == KD - 1)
                ins.then_inc(unit_done.sem, 1)

            def linear(stg, T, ready=None, squares=None, ada=None, tail=None, behind=None):
                for i in range(stg["units"]):
                    u, g = stg["u0"] + i, stg["g0"] + i
                    begin(u, g)
                    two_tiles(u, g % 2, lambda t, k: 2 * P * k + P * t, T, ready if i == 0 else None)
                    if i == 0 and tail is not None:
                        ada_sums(tail)
                    complete = ada_of_unit(ada, i)[1]
                    if complete is not None:
                        ada_sums(complete)
                    if behind:
                        behind(i)
                    if squares and i:
                        for k in (2 * i - 2, 2 * i - 1):
                            mean_square(squares, k, k % 2, T, k == 0, False)

            def ada_sums(j):
                pe.wait_ge(ada_mac.sem, 16 * j + 16)
                need(pe, mod_done, j)
                for t in range(ADA_COLS // P):
                    for v in range(2):
                        ins = mm(ps[:, 4, 2 * t + v:2 * t + v + 1], ada_acc[:, v, P * t:P * t + P], one, start=True, stop=True)
                ins.then_inc(ada_sum.sem, 1)

            def ffn_up(stg, T, n_units, ready, ada, behind_second=None):
                first, per = ADA[ada] if ada else (0, 0)
                plan = ada_plan(per)

                def step(i, j, work):
                    begin(stg["u0"] + 4 * i + j, stg["g0"] + 4 * i + j)
                    two_tiles(stg["u0"] + j, (stg["g0"] + j) % 2, lambda t, k: 8 * P * t + P * k, T,
                              ready if isinstance(i, int) and i == 0 and j == 0 else None)
                    if behind_second and isinstance(i, int) and i == 0 and j == 1:
                        behind_second()
                    if work and plan[j][1] is not None:
                        c = first + per * i + plan[j][1]
                        if not (isinstance(c, int) and c < first):
                            ada_sums(c)

                def body(i):
                    for j in range(4):
                        step(i, j, True)
                nb = n_units // 4
                repeat(pe, nb, body)
                if ada and n_units % 4 == 0:
                    ada_sums(first + per * nb - 1)
                for j in range(n_units % 4):
                    step(nb, j, False)
                    if j == 0 and ada:
                        ada_sums(first + per * nb - 1)

            def ffn_down(stg, sig, T, kt2, hi, lo, n_hidden, ada, squares, T_sq):
                first, per = ADA[ada] if ada else (0, 0)
                plan = ada_plan(per)

                def body(i):
                    for j in range(4):
                        begin(stg["u0"] + 4 * i + j, stg["g0"] + 2 * i + j // 2 if j % 2 == 0 else None)
                        if isinstance(i, int) and i == 0 and j < 2:
                            need(pe, sig["lo"], kt2 * (j + 1))
                        g, slot = (stg["g0"] + j // 2) % 2, (stg["u0"] + j) % 2
                        products(ps[:, 2 * g, 0:T], slot, [P * k for k in range(kt2)],
                                 rows_of(hi, lo, kt2 * (j % 2), kt2, T), T, j % 2 == 0, j % 2 == 1).then_inc(unit_done.sem, 1)
                        k = 2 * i + (j - 1) // 2 - 1
                        if j % 2 and not (isinstance(k, int) and k < 0):
                            mean_square(squares, k, (j // 2 + 1) % 2, T_sq, isinstance(k, int) and k == 0, False)
                        if plan[j][1] is not None:
                            c = first + per * i + plan[j][1]
                            if not (isinstance(c, int) and c < first):
                                ada_sums(c)
                repeat(pe, 4, body)
                if ada:
                    ada_sums(first + per * 4 - 1)

            pe.wait_ge(ld_rows, 16 * N_ROWS)
            turn(ps[:, 0, 0:VEC_ROWS], vec_rows[:, :], VEC_ROWS).then_inc(turned.sem, 1)
            pe.wait_ge(ld_x, 48)
            for k in range(KD):
                ins = turn(ps[:, 1, 16 * k:16 * k + 16], meta_rows[:, P * k:P * k + P], N_META)
            ins.then_inc(turned.sem, 1)
            for b in range(4):
                for k in (2 * b, 2 * b + 1):
                    for t in range(2):
                        ins = turn(ps[:, 2 + b, 256 * (k % 2) + P * t:256 * (k % 2) + P * t + P], x_rows[:, t, P * k:P * k + P], P)
                if b != 2:
                    ins.then_inc(turned.sem, 1)
            for b in range(4):
                if b >= 2:
                    pe.wait_ge(rows_out.sem, rows_out.at(5 + b - 1))
                for k in (2 * b, 2 * b + 1):
                    for t in range(2):
                        ins = turn(ps[:, 6 + b % 2, 256 * (k % 2) + P * t:256 * (k % 2) + P * t + P], ctx_rows[:, t, P * k:P * k + P], P)
                ins.then_inc(turned.sem, 1)
            pe.wait_ge(rows_out.sem, rows_out.at(1))
            for l in range(2):
                ins = turn(ps[:, 0, 72 * l:72 * l + 72], bada_rows[:, l, :], 72)
            ins.then_inc(turned.sem, 1)
            pe.wait_ge(rows_out.sem, rows_out.at(12))
            norm("mix1", T1)
            linear(st_in1, T1, norm_of["mix1"]["lo"], ada="in1")

            pe.wait_ge(ev["low_split"], 1)
            for k in range(KD):
                for w, m in ((glr_hi, u_hi), (glr_hi, u_lo), (glr_lo, u_hi)):
                    ins = mm(ps[:, 4, 0:T1], w[:, k, :], m[:, k, 0:T1], start=(k == 0 and w is glr_hi and m is u_hi),
                             stop=(k == KD - 1 and w is glr_lo))
            ins.then_inc(ev["low_sum"], 1)
            pe.wait_ge(ev["low_out"], 1)
            for t in range(2):
                ins = mm(ps[:, 4 + t, 0:T1], wgu[:, P * t:P * t + P], glr[0:16, :], start=True, stop=True)
            ins.then_inc(ev["z_sum"], 1)
            pe.wait_ge(ev["windows"], 1)
            pe.wait_ge(ev["b_sum"], 1)
            for g, w in enumerate((win_b, win_a, win_b, win_a)):
                mm(ps[:, 4 + g, 0:T1], poolw[:, g, :], w[:, g, PAD:PAD + T1], start=True, stop=True).then_inc(ev["pooled_sum"], 1)
            pe.wait_ge(ev["keys"], 1)
            pe.wait_ge(acc_free.sem, 8)
            for n, (c0, L) in enumerate(CHUNKS):
                if n >= 2:
                    pe.wait_ge(ev["chunk_rows"], n - 1)
                for h in range(4):
                    turn(ps[0:L, 2 * (n % 2), P * h:P * h + P], proj1[:, 8 + h, c0:c0 + L], P)
                for t in range(2):
                    ins = turn(ps[0:L, 1 + 2 * (n % 2), P * t:P * t + P], kend[:, t, c0:c0 + L], P)
                ins.then_inc(ev["chunk_turned"], 1)
            for n, (c0, L) in enumerate(CHUNKS):
                if n == 0:
                    pe.wait_ge(ev["pooled_out"], 4)
                if n >= 1:
                    pe.wait_ge(ev["scores_out"], n)
                if n >= 2:
                    pe.wait_ge(ev["state"], n - 1)
                pe.wait_ge(ev["chunk_rows"], n + 1)
                for h in range(4):
                    ins = mm(ps[0:L, 6, HD * h:HD * h + L], kt[:, h // 2, c0:c0 + L], qz[:, h, c0:c0 + L],
                             start=True, stop=True)
                ins.then_inc(ev["scores"], 1)
                if n < len(CHUNKS) - 1:
                    for h in range(4):
                        ins = mm(ps[:, 4 + n % 2, P * h:P * h + P], k_tok[0:L, n, P * (h // 2):P * (h // 2) + P],
                                 v_tok[0:L, n, P * h:P * h + P], start=True, stop=True)
                    ins.then_inc(ev["chunk_state"], 1)
                pe.wait_ge(ev["causal"], n + 1)
                if n:
                    pe.wait_ge(ev["state"], n)
                if n:
                    pe.wait_ge(ev["o_out"], n)
                for h in range(4):
                    ins = mm(ps[:, 7, HD * h:HD * h + L], v_tok[0:L, n, P * h:P * h + P], sT[0:L, n % 2, h, 0:L],
                             start=True, stop=(n == 0))
                    if n:
                        ins = mm(ps[:, 7, HD * h:HD * h + L], S[:, h, :], qz[:, h, c0:c0 + L], start=False, stop=True)
                ins.then_inc(ev["o_sum"], 1)
            pe.wait_ge(ev["o_sq"], 1)
            for h in range(4):
                ins = mm(ps[:, h, 0:T1], ones_d, proj1[:, h, :], start=True, stop=True)
            ins.then_inc(ev["o_ms"], 1)
            pe.wait_ge(ev["o_root"], 4)
            linear(st_out1, T1, y_ready[0], squares="ffn1")

            norm("ffn1", T1, KD - 2)
            pe.wait_ge(ev["r_split"], 1)
            nl = norm_of["ffn1"]["lo"]
            for k in range(KD):
                pe.wait_ge(nl.sem, nl.at(k + 1))
                for w, m in ((wr_hi, u_hi), (wr_lo, u_hi), (wr_hi, u_lo)):
                    ins = mm(ps[0:20, 6, 0:T1], w[:, k, :], m[:, k, 0:T1],
                             start=(k == 0 and w is wr_hi and m is u_hi), stop=(k == KD - 1 and m is u_lo))
            ins.then_inc(ev["logits"], 1)
            pe.wait_ge(ev["logits_out"], 1)
            for t, c0 in enumerate((0, P, T1 - P)):
                ins = turn(ps[:, 7, 20 * t:20 * t + 20], lgT[:, c0:c0 + P], 20)
            ins.then_inc(ev["logits_turned"], 1)

            def route():
                pe.wait_ge(ev["shares"], 1)
                for t in range(3):
                    ins = turn(ps[0:16, 7, P * t:P * t + P], r16[:, t, :], P)
                ins.then_inc(ev["shares_turned"], 1)
                pe.wait_ge(ev["shares_out"], 1)
                for e in range(N_EXPERTS):
                    if e >= 4:
                        pe.wait_ge(ev["share_out_odd" if e % 2 else "share_out"], (e - 4) // 2 + 1)
                    row_e = pick[:, e:e + 1].to_broadcast([16, P])
                    mm(ps[:, 4 + e % 4, 0:T1], row_e, comb_hi[:, :], start=True, stop=False)
                    mm(ps[:, 4 + e % 4, 0:T1], row_e, comb_lo[:, :], start=False, stop=True).then_inc(ev["share_sum"], 1)

            ffn_up(st_moe_a, T1, MOE_F, None, None, behind_second=route)
            ffn_down(st_moe_b, moe_sig, T1, 16, hm_hi, hm_lo, MOE_F, "moe_b", "end1", SEQ)
            norm("end1", SEQ, KD - 1)
            for l in range(2):
                L, A = layers[l], attn[l]
                last = l == 1
                TQ = SEQ if last else T2
                norm(f"l{l}a", T2, KD - 1 if last else 0)
                ffn_up(L["f1a"], T2, FFN_F, norm_of[f"l{l}a"]["lo"], "l1_f1a" if last else "f1a")
                ffn_down(L["f1b"], L["sig"][0], T2, 11, hf_hi, hf_lo, FFN_F, None if last else "f1b", f"l{l}b", T2)
                norm(f"l{l}b", T2, KD - 1)
                linear(L["q"], TQ, norm_of[f"l{l}b"]["lo"], ada=None if last else "q")

                def pre_work(i):
                    for x in PRE.get(i, []):
                        what, t = x
                        n, bank = PRE_ORDER.index(x), pre_bank(x)
                        if n == 0:
                            pe.wait_ge(ld_att, (l + 1) * 32)
                        if n >= 3:
                            if PRE_ORDER[n - 3][0] == "rope":
                                pe.wait_ge(A["rot"].sem, A["rot"].at(pre_count(("rope",), n - 2)))
                            else:
                                pe.wait_ge(A["pre_act"].sem, A["pre_act"].at(pre_count(("norm", "value"), n - 2)))
                        pe.wait_ge(acc_free.sem, acc_free.at(L["kv"]["g0"] + taken_with(t)))
                        if what == "norm":
                            pe.wait_ge(A["pre_sq"].sem, A["pre_sq"].at(NORM_TILES.index(t) + 1))
                            Tn = T2 if t == KB else TQ
                            ins = mm(ps[:, bank, 0:Tn], bd, tmp_b[:, NORM_TILES.index(t) % 2, 0:Tn], start=True, stop=True)
                        elif what == "rope":
                            if t in NORM_TILES:
                                pe.wait_ge(A["normed"].sem, A["normed"].at(NORM_TILES.index(t) + 1))
                            ins = mm(ps[:, bank, 0:SEQ], rot, proj2[:, t, 0:SEQ], start=True, stop=True)
                        else:
                            for j in range(4):
                                ins = turn(ps[:, bank, P * j:P * j + P], proj2[:, t, P * j:P * j + P], P)
                        ins.then_inc(A["pre_pe"].sem, 1)

                linear(L["kv"], T2, tail=None if last else 15, behind=pre_work)
                pre_work(5)
                pe.wait_ge(ld_bias, (l + 1) * 16 * GRID_H * C_HEADS)
                for i in range(6):
                    if i == 5:
                        pe.wait_ge(A["bias_out"].sem, A["bias_out"].at(1))
                    mm(ps[:, BIAS_BANKS[i], :], mirror, bias_rev[:, i // 3, 512 * (i % 3):512 * (i % 3) + 512],
                       start=True, stop=True).then_inc(A["bias"].sem, 1)
                pe.wait_ge(A["bias_out"].sem, A["bias_out"].at(6))
                pe.wait_ge(A["pre_act"].sem, A["pre_act"].at(8))
                pe.wait_ge(A["k_sw"].sem, A["k_sw"].at(1))

                def scores(i):
                    n, q0, k0, nk = A["items"][i]
                    off = HD * (n % 2)
                    if i >= 2:
                        pe.wait_ge(A["exped"].sem, A["exped"].at(i - 1))
                    for q in range(2):
                        c = q0 + P * q
                        ins = mm(ps[:, 2 * (i % 2) + q, 0:nk], proj2[off:off + HD, n // 2, c:c + P],
                                 key_tile(n)[:, k0:k0 + nk], start=True, stop=True)
                    ins.then_inc(A["scores"].sem, 1)

                def turns(i):
                    n, q0, k0, nk = A["items"][i]
                    x = i % 2
                    pe.wait_ge(A["probs"].sem, A["probs"].at(i + 1))
                    if i >= 1:
                        pe.wait_ge(A["pt"].sem, A["pt"].at(i))
                    for j in range(nk // P):
                        for q in range(2):
                            ins = turn(ps[:, 4 + j // 2, 256 * (j % 2) + P * q:256 * (j % 2) + P * q + P],
                                       s[:, x, q, P * j:P * j + P], P)
                    ins.then_inc(A["turned"].sem, 1)

                def values(i):
                    n, q0, k0, nk = A["items"][i]
                    x, off = i % 2, HD * (n % 2)
                    pe.wait_ge(A["pt"].sem, A["pt"].at(i + 1))
                    if i >= 2:
                        pe.wait_ge(A["ylo"].sem, A["ylo"].at(i - 1))
                    for j in range(nk // P):
                        ins = mm(ps[off:off + HD, 6 + x, 0:256], value_cols(n, k0 // P + j), pT[:, x, j, :],
                                 start=(j == 0), stop=(j == nk // P - 1))
                    ins.then_inc(A["o"].sem, 1)

                N = len(A["items"])
                scores(0)
                scores(1)
                for i in range(N + 1):
                    if i < N:
                        turns(i)
                    if i + 2 < N:
                        scores(i + 2)
                    if i >= 1:
                        values(i - 1)
                pe.wait_ge(A["ylo"].sem, A["ylo"].at(N))
                linear(L["out"], TQ, squares=f"l{l}c", ada=None if last else "out")
                norm(f"l{l}c", TQ, KD - 2)
                ffn_up(L["f2a"], TQ, FFN_F, norm_of[f"l{l}c"]["lo"], None if last else "f2a")
                ffn_down(L["f2b"], L["sig"][1], TQ, 11, hf_hi, hf_lo, FFN_F, None if last else "f2b",
                         "end2" if last else "l1a", TQ)
            norm("end2", SEQ, KD - 1)
            src = h2
            w = norm_of["end2"]["w"]
            pe.wait_ge(w.sem, w.at(8))
            for t in range(4):
                for k in range(4):
                    kk = 4 * (t % 2) + k
                    c = P * (t // 2)
                    ins = turn(ps[:, 2 + t, P * k:P * k + P], src[:, kk, c:c + P], P)
                ins.then_inc(turned.sem, 1)


_INS = ["x", "meta_tokens", "norm_mix_w", "w_in", "w_gate_up", "b_gate", "gla_norm_w", "pool_w", "pool_scale", "w_out",
        "norm_ffn_w", "w_router_group", "b_router_group", "w_router_expert", "b_router_expert", "w_expert_gate",
        "w_expert_up", "w_expert_down", "final_norm_w", "c_2", "ctx_2", "c_ctx_2", "w_ada_2", "b_ada_2", "norm_ffn1_2",
        "w_ffn1_gate_2", "w_ffn1_up_2", "w_ffn1_down_2", "norm_mix_2", "w_in_2", "q_norm_glob_2", "k_norm_glob_2",
        "sink_win_2", "rpb_nbr_2", "w_out_2", "norm_ffn2_2", "w_ffn2_gate_2", "w_ffn2_up_2", "w_ffn2_down_2",
        "norm_final_2"]


def kernel(**inputs):
    import concourse.bacc as bacc
    from concourse.bass_utils import run_bass_kernel_spmd

    nc = bacc.Bacc("TRN2", target_bir_lowering=False, num_devices=1, dynamic_dma_scratch_size=1024)
    arrays, a = {}, {}

    def given(name, x):
        x = np.ascontiguousarray(x)
        arrays[f"in_{name}"] = x
        a[name] = nc.dram_tensor(f"in_{name}", x.shape, F32, kind="ExternalInput").ap()

    for name in _INS:
        given(name, inputs[name])
    for name, table in zip(("base", "att", "cnt"), shape_constants()):
        given(name, table)
    out = nc.dram_tensor("out", (1, SEQ, D), F32, kind="ExternalOutput").ap()

    def by_rows(x):
        flat = x
        while len(flat.shape) > 1:
            dims = "abcd"[:len(flat.shape)]
            flat = flat.rearrange(" ".join(dims) + " -> (" + " ".join(dims) + ")")
        return flat.rearrange("(r c) -> r c", c=P)

    a["vec_src"] = [(n, by_rows(a[k])) for n, k in (
        ("c", "c_2"), ("c_ctx", "c_ctx_2"), ("norm_mix", "norm_mix_w"), ("norm_ffn", "norm_ffn_w"), ("final", "final_norm_w"),
        ("pool_scale", "pool_scale"), ("gla_norm", "gla_norm_w"), ("b_gate", "b_gate"), ("ffn1", "norm_ffn1_2"),
        ("mix", "norm_mix_2"), ("ffn2", "norm_ffn2_2"), ("final2", "norm_final_2"))]
    a["vec_src"] += [("q_norm", a["q_norm_glob_2"]), ("k_norm", a["k_norm_glob_2"])]
    program(nc, a, out)
    got = run_bass_kernel_spmd(nc, [arrays], core_ids=[0])
    return got.results[0]["out"]
```
